# Optimizing a Trainium2 kernel written in Bass

```python
import jax, jax.numpy as jnp
from jax import lax
import numpy as np

D_MODEL = 1024
BATCH = 1
SEQ = 1024
DEPTH = 1

CHUNK = 64
C_CONV = 512
CONV_WIDTH = 31
N_HEADS = 8
HEAD_DIM = 64
D_ATTN = N_HEADS * HEAD_DIM
IDX_HEADS = 8
IDX_DIM = 64
TOPK_KEYS_MAX = 256
Q_BLOCK = 128
ROPE_THETA = 10000.0
D_MIX = C_CONV + D_ATTN
N_IN = 2 * C_CONV + 3 * D_ATTN + IDX_HEADS * IDX_DIM + IDX_DIM + IDX_HEADS
N_EXPERTS = 32
TOP_K_EXPERTS = 4
D_EXPERT = 1024
SWIGLU_LIMIT = 7.0
SWIGLU_ALPHA = 1.702
EXPERT_BLOCK = 128
NORM_EPS = 1e-5

kernel_name = 'hymba_conformer_dsa_moe_block'

def rmsnorm(x, g):
    xf = x.astype(jnp.float32)
    y = xf * lax.rsqrt(jnp.mean(xf * xf, axis=-1, keepdims=True) + NORM_EPS)
    return (y * g.astype(jnp.float32)).astype(x.dtype)

def layernorm(x, g, b):
    xf = x.astype(jnp.float32)
    mu = jnp.mean(xf, axis=-1, keepdims=True)
    var = jnp.mean(jnp.square(xf - mu), axis=-1, keepdims=True)
    y = (xf - mu) * lax.rsqrt(var + NORM_EPS)
    return (y * g.astype(jnp.float32) + b.astype(jnp.float32)).astype(x.dtype)

def rope(x, pos):
    d = x.shape[-1]
    half = d // 2
    inv = ROPE_THETA ** (-jnp.arange(half, dtype=jnp.float32) / half)
    ang = pos.astype(jnp.float32)[..., None] * inv
    ang = ang.reshape(ang.shape[:2] + (1,) * (x.ndim - 3) + (half,))
    cos, sin = jnp.cos(ang), jnp.sin(ang)
    xf = x.astype(jnp.float32)
    x1, x2 = xf[..., :half], xf[..., half:]
    return jnp.concatenate([x1 * cos - x2 * sin, x2 * cos + x1 * sin], axis=-1).astype(x.dtype)

def causal_depthwise_conv(u, w, b):
    out = lax.conv_general_dilated(
        u, w[:, None, :].astype(u.dtype), window_strides=(1,),
        padding=[(CONV_WIDTH - 1, 0)], dimension_numbers=('NWC', 'WIO', 'NWC'),
        feature_group_count=u.shape[-1])
    return out + b.astype(u.dtype)

def dsa_attention(q, k, v, qi, ki, wi, pos):
    B, S = pos.shape
    nb = S // Q_BLOCK
    k_sel = min(TOPK_KEYS_MAX, S // 4)
    chunk = pos // CHUNK
    gather = jax.vmap(lambda a, i: a[i])

    def to_blocks(a):
        return jnp.moveaxis(a.reshape((B, nb, Q_BLOCK) + a.shape[2:]), 1, 0)

    def one_block(args):
        qb, qib, wib, cqb = args
        s_h = jax.nn.relu(jnp.einsum('bqhd,bsd->bqhs', qib, ki).astype(jnp.float32))
        s_idx = jnp.einsum('bqhs,bqh->bqs', s_h, wib.astype(jnp.float32))
        adm = chunk[:, None, :] <= cqb[:, :, None]
        s_idx = jnp.where(adm, s_idx, -jnp.inf)
        _, sel = lax.top_k(s_idx, k_sel)
        kg = gather(k, sel)
        vg = gather(v, sel)
        valid = gather(chunk, sel) <= cqb[:, :, None]
        logits = jnp.einsum('bqhd,bqkhd->bqhk', qb, kg).astype(jnp.float32) * (HEAD_DIM ** -0.5)
        logits = jnp.where(valid[:, :, None, :], logits, -jnp.inf)
        p = jax.nn.softmax(logits, axis=-1).astype(vg.dtype)
        return jnp.einsum('bqhk,bqkhd->bqhd', p, vg)

    out = lax.map(one_block, (to_blocks(q), to_blocks(qi), to_blocks(wi), to_blocks(chunk)))
    return jnp.moveaxis(out, 0, 1).reshape(B, S, -1)

def moe_ffn(xn, w_router, b_router, w_gate_up, b_gate_up, w_down, b_down):
    B, S, D = xn.shape
    T = B * S
    xf = xn.reshape(T, D)
    logits = (xf @ w_router + b_router).astype(jnp.float32)
    top_vals, top_idx = lax.top_k(logits, TOP_K_EXPERTS)
    gates = jax.nn.softmax(top_vals, axis=-1)
    n_pairs = T * TOP_K_EXPERTS
    expert_flat = top_idx.reshape(-1).astype(jnp.int32)
    token_flat = jnp.arange(n_pairs, dtype=jnp.int32) // TOP_K_EXPERTS
    gate_flat = gates.reshape(-1)
    order = jnp.argsort(expert_flat, stable=True)
    sorted_expert = expert_flat[order]
    counts = jax.ops.segment_sum(jnp.ones_like(expert_flat), expert_flat, num_segments=N_EXPERTS)
    padded = (counts + EXPERT_BLOCK - 1) // EXPERT_BLOCK * EXPERT_BLOCK
    start = jnp.cumsum(counts) - counts
    padded_end = jnp.cumsum(padded)
    padded_start = padded_end - padded
    dest = padded_start[sorted_expert] + jnp.arange(n_pairs, dtype=jnp.int32) - start[sorted_expert]
    n_blocks = -(-n_pairs // EXPERT_BLOCK) + N_EXPERTS
    n_rows = n_blocks * EXPERT_BLOCK
    row_token = jnp.zeros((n_rows,), jnp.int32).at[dest].set(token_flat[order])
    row_gate = jnp.zeros((n_rows,), jnp.float32).at[dest].set(gate_flat[order])
    block_start = jnp.arange(n_blocks, dtype=jnp.int32) * EXPERT_BLOCK
    block_expert = jnp.minimum(jnp.searchsorted(padded_end, block_start, side='right'), N_EXPERTS - 1)

    def expert_block(args):
        xb, e = args
        gu = xb @ w_gate_up[e] + b_gate_up[e]
        g, u = jnp.split(gu, 2, axis=-1)
        g = jnp.minimum(g, SWIGLU_LIMIT)
        u = jnp.clip(u, -SWIGLU_LIMIT, SWIGLU_LIMIT)
        hdn = g * jax.nn.sigmoid(SWIGLU_ALPHA * g) * (u + 1)
        return hdn @ w_down[e] + b_down[e]

    xs = xf[row_token].reshape(n_blocks, EXPERT_BLOCK, D)
    ys = lax.map(expert_block, (xs, block_expert)).reshape(n_rows, D)
    ys = ys * row_gate[:, None].astype(ys.dtype)
    out = jnp.zeros_like(xf).at[row_token].add(ys)
    return out.reshape(B, S, D)

def setup_inputs(seed: int = 0) -> dict:
    key = jax.random.key(seed)
    ks = jax.random.split(key, 20)
    f32 = jnp.float32

    def nrm(k, shape, scale):
        return jax.random.normal(k, shape, f32) * scale

    return {
        'x': nrm(ks[0], (BATCH, SEQ, D_MODEL), 1.0),
        'positions': jnp.broadcast_to(jnp.arange(SEQ, dtype=jnp.int32), (BATCH, SEQ)),
        'norm_mix_g': 1.0 + nrm(ks[1], (DEPTH, D_MODEL), 0.02),
        'w_in': nrm(ks[2], (DEPTH, D_MODEL, N_IN), D_MODEL ** -0.5),
        'idx_k_norm_g': 1.0 + nrm(ks[3], (DEPTH, IDX_DIM), 0.02),
        'idx_k_norm_b': nrm(ks[4], (DEPTH, IDX_DIM), 0.02),
        'conv_w': nrm(ks[5], (DEPTH, CONV_WIDTH, C_CONV), CONV_WIDTH ** -0.5),
        'conv_b': nrm(ks[6], (DEPTH, C_CONV), 0.02),
        'conv_norm_g': 1.0 + nrm(ks[7], (DEPTH, C_CONV), 0.02),
        'conv_norm_b': nrm(ks[8], (DEPTH, C_CONV), 0.02),
        'w_out': nrm(ks[9], (DEPTH, D_MIX, D_MODEL), D_MIX ** -0.5),
        'norm_ffn_g': 1.0 + nrm(ks[10], (DEPTH, D_MODEL), 0.02),
        'w_router': nrm(ks[11], (DEPTH, D_MODEL, N_EXPERTS), D_MODEL ** -0.5),
        'b_router': nrm(ks[12], (DEPTH, N_EXPERTS), 0.01),
        'w_gate_up': nrm(ks[13], (DEPTH, N_EXPERTS, D_MODEL, 2 * D_EXPERT), D_MODEL ** -0.5),
        'b_gate_up': nrm(ks[14], (DEPTH, N_EXPERTS, 2 * D_EXPERT), 0.01),
        'w_down': nrm(ks[15], (DEPTH, N_EXPERTS, D_EXPERT, D_MODEL), D_EXPERT ** -0.5),
        'b_down': nrm(ks[16], (DEPTH, N_EXPERTS, D_MODEL), 0.01),
        'norm_final_g': 1.0 + nrm(ks[17], (D_MODEL,), 0.02),
    }

def reference(x, positions, norm_mix_g, w_in, idx_k_norm_g, idx_k_norm_b, conv_w, conv_b,
              conv_norm_g, conv_norm_b, w_out, norm_ffn_g, w_router, b_router, w_gate_up,
              b_gate_up, w_down, b_down, norm_final_g):
    B, S, _ = x.shape
    sizes = (C_CONV, C_CONV, D_ATTN, D_ATTN, D_ATTN, IDX_HEADS * IDX_DIM, IDX_DIM, IDX_HEADS)
    cuts = [sum(sizes[:i + 1]) for i in range(len(sizes) - 1)]
    h = x
    for l in range(DEPTH):
        hn = rmsnorm(h, norm_mix_g[l])
        proj = hn @ w_in[l]
        glu_val, glu_gate, q, k, v, qi, ki, wi = jnp.split(proj, cuts, axis=-1)
        u = glu_val * jax.nn.sigmoid(glu_gate)
        u = causal_depthwise_conv(u, conv_w[l], conv_b[l])
        u = jax.nn.silu(layernorm(u, conv_norm_g[l], conv_norm_b[l]))
        q = rope(q.reshape(B, S, N_HEADS, HEAD_DIM), positions)
        k = rope(k.reshape(B, S, N_HEADS, HEAD_DIM), positions)
        v = v.reshape(B, S, N_HEADS, HEAD_DIM)
        qi = rope(qi.reshape(B, S, IDX_HEADS, IDX_DIM), positions)
        ki = rope(layernorm(ki, idx_k_norm_g[l], idx_k_norm_b[l]), positions)
        wi = wi * (IDX_HEADS ** -0.5 * IDX_DIM ** -0.5)
        a = dsa_attention(q, k, v, qi, ki, wi, positions)
        h = h + jnp.concatenate([u, a], axis=-1) @ w_out[l]
        h = h + moe_ffn(rmsnorm(h, norm_ffn_g[l]), w_router[l], b_router[l], w_gate_up[l],
                        b_gate_up[l], w_down[l], b_down[l])
    return rmsnorm(h, norm_final_g)


_drawn_inputs = setup_inputs


def setup_inputs(seed=0):
    import zlib

    import numpy as np

    out = dict(_drawn_inputs(seed))
    spreads = {}
    factors = {'idx_k_norm_g': 2.787,
     'idx_k_norm_b': 2.881,
     'b_gate_up': 8.0,
     'b_down': 8.0,
     'norm_final_g': 2.876}
    for name, (base, spread) in spreads.items():
        noise = np.random.default_rng([zlib.crc32(name.encode()), seed]).standard_normal(out[name].shape)
        drawn = base * np.exp(spread * noise) if base else spread * noise
        out[name] = __import__('jax').numpy.asarray(drawn.astype(out[name].dtype))
    for name, factor in factors.items():
        out[name] = (out[name] * factor).astype(out[name].dtype)
    return out
```

```python
from contextlib import ExitStack

import numpy as np

import concourse.bass as bass
from concourse import mybir

ALU = mybir.AluOpType
ACT = mybir.ActivationFunctionType
AX = mybir.AxisListType.X
F32 = mybir.dt.float32
BF16 = mybir.dt.bfloat16
F16 = mybir.dt.float16
I32 = mybir.dt.int32
U32 = mybir.dt.uint32

P = 128
SEQ = 1024
D = 1024
KD = D // P
NT = SEQ // P
CHUNK_SHIFT = 6
C_CONV = 512
CC = C_CONV // P
TAPS = 31
PAD = TAPS - 1
HEADS = 8
HD = 64
HALF_HD = HD // 2
D_ATTN = HEADS * HD
PAIRS = HEADS // 2
TOPK = 256
NE = 32
TOPE = 4
FE = 1024
FJ = FE // P
EPS = 1e-5
LIMIT = 7.0
ALPHA = 1.702
WI_SCALE = HEADS ** -0.5 * HD ** -0.5
THETA = 10000.0
NOT_ADMITTED = -3.0e38
MASKED = -(2.0 ** 100)
C_Q, C_K, C_V = 2 * C_CONV, 2 * C_CONV + D_ATTN, 2 * C_CONV + 2 * D_ATTN
C_QI = 2 * C_CONV + 3 * D_ATTN
C_KI = C_QI + D_ATTN
N_KI = HD + HEADS

CAP = 192
CAP2 = CAP - P
CONV_AHEAD = {False: (0, 10, 10), True: (40, 2, 8)}
ROUNDS = -(-SEQ // CAP)
WIDTHS = tuple(range(128, CAP + 1, 16))
EXTRA = SEQ * TOPE // CAP
SLOT_COLS = 5
LIST_AT = (2 * CAP, 2 * CAP + 8)

K_IDENT, K_UPPER, K_IOTA, K_INV, K_TOK = 0, 128, 256, 448, 480
K_COLS = K_TOK + 2 * NT

TWO_PI = 2 * np.pi
PI_A = 6.28125
PI_B = float(np.float32(np.floor((TWO_PI - PI_A) * 2 ** 21) / 2 ** 21))
PI_C = float(np.float32(TWO_PI - PI_A - PI_B))
ROUND_MAGIC = 12582912.0
PI_SAFE = 3.1415925


def build(nc, x, positions, norm_mix_g, w_in, idx_k_norm_g, idx_k_norm_b, conv_w, conv_b,
          conv_norm_g, conv_norm_b, w_out, norm_ffn_g, w_router, b_router, w_gate_up, b_gate_up,
          w_down, b_down, norm_final_g, consts, head_rows, out):
    ctx = ExitStack()
    with ctx:
        arena = ctx.enter_context(nc.sbuf_tensor("arena", [P, 53120], F32))
        ps = ctx.enter_context(nc.psum_tensor("ps", [P, 8, 512], F32))
        xn_dram = nc.dram_tensor("xn_scratch", (SEQ + 1, D), F32, kind="Internal").ap()
        h_dram = nc.dram_tensor("h_scratch", (SEQ + 1, D), F32, kind="Internal").ap()

        def sem(name):
            return ctx.enter_context(nc.semaphore(name))

        def at(byte, shape, dt=F32, rows=(0, P)):
            size = mybir.dt.size(dt)
            n = int(np.prod(shape)) * size
            assert byte % 4 == 0 and byte + n <= 53120 * 4
            words = arena[rows[0]:rows[1], byte // 4:byte // 4 + -(-n // 4)]
            v = words if dt == F32 else words.bitcast(dt)
            if n % 4:
                v = v[:, 0:int(np.prod(shape))]
            if len(shape) == 1:
                return v
            names = " ".join("abcd"[:len(shape)])
            return v.rearrange(f"p ({names}) -> p {names}", **dict(zip("abcd", shape)))

        HNT = 0
        WB = [32768, 49152]
        SC = 65536
        QT, KT, VV, MT, CB, SM = 98304, 114688, 131072, 155648, 172032, 193152
        hnT = at(HNT, [KD, SEQ])
        wbuf = [at(WB[b], [KD, 512]) for b in range(2)]
        wki = at(WB[1], [KD, N_KI])
        x_sb = at(SC, [NT, D])
        score = at(SC, [NT, SEQ])
        maskq = [at(SC + 4096 * t, [SEQ], BF16) for t in range(NT)]
        wout = at(SC, [KD, D])
        q_pad = [at(QT, [PAIRS, SEQ]), at(WB[1], [PAIRS, SEQ])]
        kT = at(KT, [PAIRS, SEQ])
        vv = at(VV, [NT, PAIRS, 192])
        qiT = at(MT, [PAIRS, SEQ])
        w_kvq = [at(MT, [KD, 512]), wbuf[1], wbuf[0]]
        maskT = at(MT, [NT, SEQ], BF16)
        SLOT = 1056
        cslot = [at(CB + 4 * SLOT * i, [SLOT]) for i in range(5)]
        chunk_row = at(QT, [SEQ])
        relu_buf = [at(QT + 4096 + 4096 * b, [SEQ]) for b in range(2)]
        pos_row = at(QT + 12288, [SEQ], I32)
        kiw = at(KT, [NT, N_KI])
        kin = at(KT + 2304, [NT, P])
        kit1 = at(KT + 2304 + 4096, [NT, HD])
        kit2 = at(KT + 2304 + 4096 + 2048, [NT, HD])
        ki_pad = [at(KT + 10752, [SEQ]), at(QT + 12288, [SEQ])]
        lng = at(KT + 14848, [HD])
        lnb = at(KT + 15104, [HD])
        junk_x = at(MT, [D])
        o = SM
        cos2 = at(o, [NT, HD]); o += 2048
        sin2 = at(o, [NT, HD]); o += 2048
        raw = [at(o + 2048 * b, [512]) for b in range(2)]; o += 4096
        rot = [at(o + 2048 * b, [512]) for b in range(2)]; o += 4096
        swapped = at(o, [512]); o += 2048
        ranks = at(o, [SEQ], F16)
        negmaxT = at(o, [SEQ], BF16); o += 2048
        ident = at(o, [P]); o += 512
        identb = at(o, [P], BF16); o += 256

        def col(n, dt=F32, rows=(0, P)):
            nonlocal o
            v = at(o, [n] if isinstance(n, int) else n, dt, rows)
            o += 4 * int(np.prod(n))
            return v

        gmixT, ssq, rms, rstd = col(KD), col(NT), col(NT), col(NT)
        wis = col([NT, HEADS])
        bound, bound_try = col(NT, I32), col(NT, I32)
        count, keep = col(NT), col(NT, I32)
        chunk_q = col(NT)
        rowmax = col([NT, HEADS])
        convw = col([CC, TAPS])
        convb, cng, cnb = col(CC), col(CC), col(CC)
        kis1, kis2 = col(NT), col(NT)
        chunk_tmp, eps = col(NT), col(1)
        tile_lo, tile_hi, causal_i = col(NT), col(NT), col(1, I32)
        assert o <= 53120 * 4, o
        selg = at(CB, [SEQ], BF16)
        sele = at(CB + 2048, [SEQ], BF16)
        headrow = at(SM + 4096, [HEADS, P], BF16)
        negmax = at(SM + 6144, [NT, HEADS])
        nm_rest = at(SM + 6400, [NT, HEADS])
        nm_parts = at(SM + 6656, [NT, 3, HEADS], BF16)
        ones_c = at(SM + 7168, [P])
        zero_rows = at(WB[1] + 4096, [D])
        probT = [at(HNT + 16384 * b, [NT, 512]) for b in range(2)]
        aT = at(WB[0], [PAIRS, SEQ])
        rden = swapped
        sq_buf = [at(SM + 2048 * b, [512]) for b in range(2)]
        lrstd = at(SM + 8192, [2, 512])
        sg_buf = sq_buf
        posq_i = at(MT + 4096, [NT], I32)
        posq = at(MT + 4160, [NT])
        ang = at(MT + 4352, [NT, HALF_HD])
        turn = at(MT + 5376, [NT, HALF_HD])
        ang_r = at(MT + 6400, [NT, HALF_HD])
        invf = at(MT + 7424, [HALF_HD])

        s_first = sem("identity_and_gain_loaded")
        s_small = sem("small_loaded")
        s_convp = sem("conv_parameters_loaded")
        s_xt = [sem(f"x_tile_loaded{t}") for t in range(NT)]
        s_sq = sem("squares_summed")
        s_rms = sem("rms_ready")
        s_xn = sem("x_normalised")
        s_htp = sem("hn_transposed")
        s_hnT = sem("hnT_written")
        s_w = {n: sem(f"w_in_{n}_loaded") for n in ("ki", "qi", "val", "gate", "q", "k", "v")}
        s_dve = sem("vector_step")
        s_gps = sem("gpsimd_step")
        s_proj = sem("projection_summed")
        s_raw = sem("projection_copied")
        s_trig = sem("angles_ready")
        s_sin = sem("sines_ready")
        s_kivar = sem("ki_variance")
        s_kirms = sem("ki_rms")
        s_kin = sem("ki_rotated")
        s_rotA = sem("qi_rotated")
        s_rotB = sem("qk_rotated")
        s_tp = sem("tile_transposed")
        s_tpv = sem("transpose_copied")
        s_idx = sem("index_products")
        s_relu = sem("index_relu")
        s_acc = sem("index_accumulated")
        s_glu = sem("glu_summed")
        s_gluc = sem("glu_copied")
        s_u = sem("glu_written")
        s_padz = sem("pads_zeroed")
        s_tally = sem("scores_tallied")
        s_mask = sem("mask_ready")
        s_qz = sem("padding_zeroed")
        s_kiz = sem("ki_padding_zeroed")
        s_la = sem("logits_a")
        s_mx = sem("max_taken")
        s_nm = sem("negmax_parts")
        s_lb = sem("logits_b")
        s_exp = sem("probs_ready")
        s_pv = sem("pv_step")
        s_head = sem("head_summed")
        s_causal = sem("causal_flag_ready")
        s_aT = sem("attn_written")
        s_conv = sem("conv_done")
        s_mean = sem("conv_mean")
        s_xc = sem("conv_centred")
        s_csq = sem("conv_squares")
        s_cvar = sem("conv_var")
        s_cstd = sem("conv_std")
        s_cn = sem("conv_normed")
        s_csg = sem("conv_sigmoid")
        s_uo = sem("conv_branch_ready")
        s_ident = sem("identity_bf16")
        s_wout = sem("w_out_loaded")
        s_hrow = sem("head_rows_loaded")
        s_kis = sem("eps_ready")
        s_zero = sem("zero_rows_ready")
        s_zeroed = sem("spare_rows_zeroed")

        ident_src = consts[:, K_IDENT:K_IDENT + P]
        x_t = x.rearrange("b (t p) d -> (b t) p d", p=P)
        pos_row_src = positions[0, :].partition_broadcast(P)
        win = w_in[0].rearrange("(k p) n -> p k n", p=P)

        def psb(bank, n=1):
            return ps[:, bank:bank + n, :]

        def flat(bank, n):
            return ps[:, bank:bank + n, :].rearrange("p b n -> p (b n)")

        def rotate(eng, link, src, dst, t):
            s4 = src.rearrange("p (h a c) -> p h a c", h=HEADS, a=2)
            w4 = swapped.rearrange("p (h a c) -> p h a c", h=HEADS, a=2)
            s3 = src.rearrange("p (h c) -> p h c", h=HEADS)
            d3 = dst.rearrange("p (h c) -> p h c", h=HEADS)
            cosb = cos2[:, t:t + 1, :].to_broadcast([P, HEADS, HD])
            link(eng.tensor_tensor(w4[:, :, 0, :], s4[:, :, 1, :],
                                   sin2[:, t:t + 1, 0:HALF_HD].to_broadcast([P, HEADS, HALF_HD]), ALU.mult))
            link(eng.tensor_tensor(w4[:, :, 1, :], s4[:, :, 0, :],
                                   sin2[:, t:t + 1, HALF_HD:HD].to_broadcast([P, HEADS, HALF_HD]), ALU.mult))
            link(eng.tensor_tensor(d3, s3, cosb, ALU.mult))
            return eng.tensor_tensor(dst, dst, swapped, ALU.add)

        def conv_out(c):
            return cslot[c][:, PAD:PAD + SEQ]

        def conv_view(i):
            n, c = i // CC, i % CC
            return conv_out(c)[:, 512 * n:512 * n + 512]

        def rotated(i):
            return i if i < NT else i - NT if i >= 2 * NT else None

        def either(eng, causal, body):
            with eng.If(causal == 0):
                body(False)
            eng.nop()
            with eng.If(causal == 1):
                body(True)
            eng.nop()

        def keys_of(t, causal):
            return P * (t + 1) if causal else SEQ

        def key_parts(t, causal):
            w = keys_of(t, causal)
            return [(n, 512 * n, min(512, w - 512 * n)) for n in range(2) if w > 512 * n]

        def second_pass(causal):
            blocks = []
            for g in range(2 * HEADS):
                for kt in range(NT):
                    skip = max(0, P * kt - 512 * (g // HEADS)) if causal else 0
                    if skip < 512:
                        blocks.append((g, kt, skip))
            return blocks

        h_sb = at(QT, [NT, D])
        hn2 = [at(VV + 4096 * b, [D]) for b in range(2)]
        hn2T = [at(VV + 8192 + 4096 * b, [KD, P]) for b in range(2)]
        gain2 = at(VV + 16384, [D])
        gainf = at(VV + 20480, [D])
        x_again = [at(MT + 4096 * b, [D]) for b in range(3)]
        bias_gu_rows = at(MT + 12288, [4, P])
        bias_d_rows = at(MT + 14336, [2, P])
        w_rt = at(SM, [KD, NE])
        iota = at(SM + 1024, [CAP])
        upper = at(SM + 1792, [P])
        tok = at(SM + 2304, [NT, 2])
        round_idx, round_gate = at(SM + 2368, [2], I32), at(SM + 2376, [2])
        kept_idx, kept_gate = at(SM + 2384, [2], I32), at(SM + 2392, [2])
        b_rt = at(SM + 2496, [NE])
        upperb = at(SM + 2624, [P], BF16)
        onesb = at(SM + 2880, [P], BF16)
        tokb = at(SM + 3904, [NT, 2], BF16)
        item_off = at(SM + 3200, [EXTRA])
        n_items = at(SM + 3300, [1], I32)
        token_idx, token_gate = at(SM + 3328, [2], I32), at(SM + 3336, [2])
        pos_item = at(SM + 3344, [NT])
        ssq2, rms2, rstd2, tmp2 = (at(SM + 3392 + 32 * i, [NT]) for i in range(4))
        extra_rounds = at(SM + 3520, [NE])
        extra_sum = at(SM + 3648, [NE])
        round_cmp = at(SM + 3776, [NE])
        biasT = at(SM + 4096, [NE * 2 * FJ])
        biasdT = at(SM + 6144, [NE * KD])
        ranked = at(SM + 7168, [NT, NE + 1])
        logits = at(SM + 8224, [NT, NE])
        prod = at(SM + 8224, [NT, NE])
        top8 = at(SM + 9248, [NT, 8])
        top8_i = at(SM + 9504, [NT, 8], U32)
        top8_f = at(SM + 9760, [NT, 8])
        onehot = at(SM + 10016, [TOPE, NT, NE])
        item_cmp = at(SM + 10016, [EXTRA, NE])
        member = at(SM + 14112, [NT, NE], BF16)
        gate_of = at(SM + 14624, [NT, NE])
        gate_rest = at(VV + 12288, [NT, NE])
        slot_rows = at(VV + 8192, [NT, NE + 1, SLOT_COLS], BF16)
        item_e_f = at(SM + 14624, [EXTRA])
        item_x_f = at(SM + 14720, [EXTRA])
        classes = at(SM + 8224 + 1024 + 256 + 256, [NE + 1], I32)
        gates = at(SM + 15648, [NT, TOPE])
        counts = at(SM + 16032, [NE])
        item_e = at(SM + 16160, [EXTRA], I32)
        w_gu = [at(16384 * q, [KD, 2, 256]) for q in range(4)]
        w_dn = [at(65536 + 8192 * q, [KD, 256]) for q in range(4)]
        xg = [at(CB, [D]), at(CB + 4096, [D], rows=(0, CAP2))]
        xgT = at(CB + 8192, [KD, CAP])
        hT = at(CB + 8192 + 6144, [FJ, CAP])
        h_rows = [at(MT, [D]), at(MT + 4096, [D], rows=(0, CAP2))]
        yT = [at(MT + 8192 + 768 * b, [CAP]) for b in range(2)]
        picks = at(MT + 9728, [NT, CAP], BF16)
        gmin, umin, sig, gsig = (at(MT + 12800 + 768 * b, [CAP]) for b in range(4))

        s_xr = [sem(f"x_again_loaded{b}") for b in range(3)]
        s_par = sem("router_parameters_loaded")
        s_bias = sem("bias_rows_loaded")
        s_wo = sem("mix_projected")
        s_h2 = sem("h_written")
        s_sq2 = sem("h_squares")
        s_rms2 = sem("h_rms")
        s_hn2 = sem("hn2_written")
        s_hst = [sem(f"hn2_stored{b}") for b in range(2)]
        s_h2tp = sem("hn2_transposed")
        s_h2T = sem("hn2T_written")
        s_rt = sem("router_logits")
        s_bT = sem("bias_transposed")
        s_bTc = sem("bias_copied")
        s_gexp = sem("gate_differences")
        s_gexpd = sem("gate_exps")
        s_mem = sem("membership_ready")
        s_rank = sem("ranks_summed")
        s_plan = sem("plan_ready")
        s_pick = sem("picks_ready")
        s_list = sem("token_list_summed")
        s_tok = sem("token_list_ready")
        s_gat = sem("rows_gathered")
        s_xtp = sem("rows_transposed")
        s_xgT = sem("xgT_written")
        s_wgu = [sem(f"gate_up_loaded{q}") for q in range(4)]
        s_wdn = [sem(f"down_loaded{q}") for q in range(4)]
        s_gu = sem("gate_up_summed")
        s_glm = sem("swiglu_step")
        s_sig = sem("sigmoid_ready")
        s_hid = sem("hidden_written")
        s_dn = sem("down_summed")
        s_yT = sem("yT_written")
        s_ytp = sem("y_transposed")
        s_hd = sem("h_stored")
        s_rows = sem("slot_rows_ready")
        s_listg = sem("first_gates_summed")
        s_kept = sem("list_kept")
        s_turn = sem("slots_of_round_taken")
        s_hg = sem("h_rows_gathered")
        s_add = sem("h_rows_added_to")
        s_put = sem("h_rows_put_back")
        s_free = sem("round_slots_free")
        s_gate = sem("wait_carrier")
        s_back = [sem(f"h_tile_back{t}") for t in range(NT)]
        s_sq3 = sem("final_squares")
        s_rms3 = sem("final_rms")
        s_fin = sem("final_written")
        s_out = sem("output_stored")

        N_PAR, N_BIAS = 7, 2
        wgu_src = w_gate_up[0].rearrange("e (k p) (a n) -> e p k a n", p=P, a=2)
        wdn_src = w_down[0].rearrange("e (k p) n -> e p k n", p=P)
        out_t = out.rearrange("b (t p) d -> (b t) p d", p=P)

        def load_gate_up(sp, e, q):
            for a in range(2):
                sp.dma_start(w_gu[q][:, :, a, :], wgu_src[e, :, :, a, 256 * q:256 * q + 256]).then_inc(s_wgu[q], 16)

        def load_down(sp, e, q):
            sp.dma_start(w_dn[q], wdn_src[e, :, :, 256 * q:256 * q + 256]).then_inc(s_wdn[q], 16)

        def load_expert(sp, n, e):
            for q in range(4):
                sp.wait_ge(s_gu, n * FJ + (2 * q + 2 - FJ))
                load_gate_up(sp, e, q)
            for q in range(4):
                sp.wait_ge(s_dn, n * KD + (2 * q + 2 - KD))
                load_down(sp, e, q)

        def read_index(eng, table, i, top):
            return eng.value_load(table[0:1, bass.ds(i, 1)], min_val=0, max_val=top)

        FINAL_GROUPS = [[0], [1, 2], [3, 4, 5], [6, 7]]

        def wo_banks(t):
            b = 2 * ((t + 1) % 2)
            return ps[:, b:b + 2, :]

        def moe_sync(sp):
            with nc.allow_non_contiguous_dma(reason="small parameters"):
                sp.wait_ge(s_uo, 2 * CC)
                for dst, src in ((w_rt, w_router[0].rearrange("(k p) e -> p k e", p=P)),
                                 (iota, consts[:, K_IOTA:K_IOTA + CAP]),
                                 (upper, consts[:, K_UPPER:K_UPPER + P]),
                                 (tok, consts[:, K_TOK:K_TOK + 2 * NT].rearrange("p (t a) -> p t a", a=2)),
                                 (b_rt, b_router[0].partition_broadcast(P))):
                    sp.dma_start(dst, src).then_inc(s_par, 16)
                sp.wait_ge(s_head, 2 * HEADS)
                sp.dma_start(gain2, norm_ffn_g[0].partition_broadcast(P)).then_inc(s_par, 16)
                sp.dma_start(gainf, norm_final_g.partition_broadcast(P)).then_inc(s_par, 16)
            for t in range(3):
                sp.dma_start(x_again[t], x_t[t]).then_inc(s_xr[t], 16)
            sp.dma_start(bias_gu_rows, b_gate_up[0].rearrange("(a e) (j p) -> (e j) a p", a=4, p=P)).then_inc(s_bias, 16)
            sp.dma_start(bias_d_rows, b_down[0].rearrange("(a e) (j p) -> (e j) a p", a=2, p=P)).then_inc(s_bias, 16)
            for q in range(2):
                load_gate_up(sp, 0, q)
            for t in range(NT + 2):
                if t >= 2:
                    sp.wait_ge(s_hn2, t - 1)
                    sp.dma_start(xn_dram[(t - 2) * P:(t - 1) * P, :], hn2[t % 2]).then_inc(s_hst[t % 2], 16)
                    sp.dma_start(h_dram[(t - 2) * P:(t - 1) * P, :], h_sb[:, t - 2, :]).then_inc(s_hd, 16)
                if 1 <= t and t + 2 < NT:
                    sp.wait_ge(s_h2, t)
                    sp.dma_start(x_again[(t + 2) % 3], x_t[t + 2]).then_inc(s_xr[(t + 2) % 3], 16)
                if t == NT - 1:
                    sp.wait_ge(s_wo, NT)
                    for q in range(2, 4):
                        load_gate_up(sp, 0, q)
            sp.wait_ge(s_gat, 32)
            for q in range(4):
                load_down(sp, 0, q)
            with sp.Fori(1, NE) as e:
                load_expert(sp, e, e)
            total = sp.value_load(n_items[0:1, 0:1], min_val=0, max_val=EXTRA)
            with sp.Fori(0, EXTRA) as i:
                with sp.If(total > i):
                    load_expert(sp, i + NE, read_index(sp, item_e, i, NE - 1))
                    sp.wait_ge(s_put, i * 32 + 32 * (NE + 1))
                    sp.sem_inc(s_gate, 1)
                sp.nop()
            sp.wait_ge(s_put, 32 * NE)
            for t in range(NT):
                sp.dma_start(h_sb[:, t, :], h_dram[t * P:(t + 1) * P, :]).then_inc(s_back[t], 16)
            for t in range(NT):
                sp.wait_ge(s_fin, t + 1)
                sp.dma_start(out_t[t], h_sb[:, t, :]).then_inc(s_out, 16)
            sp.wait_ge(s_out, 16 * NT)

        def moe_gpsimd(pool):
            def gather(p):
                pool.wait_ge(s_tok, 2 if isinstance(p, int) and p == 0 else 4 * p + 4)
                pool.sem_inc(s_gate, 1)
                nc.gpsimd.indirect_dma_start(xg[0], None, xn_dram, bass.IndirectOffsetOnAxis(token_idx[:, 0:1], 0)
                                             ).then_inc(s_gat, 16)
                nc.gpsimd.indirect_dma_start(xg[1], None, xn_dram,
                                             bass.IndirectOffsetOnAxis(token_idx[0:CAP2, 1:2], 0)).then_inc(s_gat, 16)

            def gather_h(n):
                pool.wait_ge(s_turn, 2 * n + 2)
                pool.sem_inc(s_gate, 1)
                nc.gpsimd.indirect_dma_start(h_rows[0], None, h_dram, bass.IndirectOffsetOnAxis(round_idx[:, 0:1], 0)
                                             ).then_inc(s_hg, 16)
                nc.gpsimd.indirect_dma_start(h_rows[1], None, h_dram,
                                             bass.IndirectOffsetOnAxis(round_idx[0:CAP2, 1:2], 0)).then_inc(s_hg, 16)

            def put_h(n):
                pool.wait_ge(s_add, 4 * n + 5)
                pool.sem_inc(s_gate, 1)
                nc.gpsimd.indirect_dma_start(h_dram, bass.IndirectOffsetOnAxis(round_idx[:, 0:1], 0), h_rows[0], None
                                             ).then_inc(s_put, 16)
                pool.wait_ge(s_put, 32 * n + 16)
                pool.sem_inc(s_gate, 1)
                nc.gpsimd.indirect_dma_start(h_dram, bass.IndirectOffsetOnAxis(round_idx[0:CAP2, 1:2], 0), h_rows[1], None
                                             ).then_inc(s_put, 16)
                pool.wait_ge(s_put, 32 * n + 32)
                pool.sem_inc(s_free, 1)

            for b in range(2):
                pool.wait_ge(s_hst[b], 8 * NT)
            pool.wait_ge(s_hd, 16 * NT)
            pool.wait_ge(s_zeroed, 32)
            gather(0)
            pool.sem_inc(s_free, 1)
            with pool.Fori(0, NE) as e:
                pool.wait_ge(s_xtp, e * 4 + 4)
                gather(e + 1)
                gather_h(e)
                put_h(e)
            total = pool.value_load(n_items[0:1, 0:1], min_val=0, max_val=EXTRA)
            with pool.Fori(0, EXTRA) as i:
                with pool.If(total > i):
                    pool.wait_ge(s_xtp, i * 4 + 4 * (NE + 1))
                    gather(i + NE + 1)
                    gather_h(i + NE)
                    put_h(i + NE)
                pool.nop()

        def moe_scalar(act):
            junk = at(SM + 10016, [D], BF16)

            def root(t, s_in, s_done):
                if s_in:
                    act.wait_ge(s_in, t + 1)
                if t:
                    act.wait_ge(s_done[1], t)
                nc.scalar.activation(junk, h_sb[:, t, :], ACT.Square, accum_out=ssq2[:, t:t + 1]).then_inc(s_done[0], 1)
                act.wait_ge(s_done[0], t + 1)
                nc.scalar.activation(rms2[:, t:t + 1], ssq2[:, t:t + 1], ACT.Sqrt, scale=1.0 / D, bias=eps
                                     ).then_inc(s_done[1], 1)

            for t in range(NT + 1):
                if t < NT:
                    root(t, s_h2, (s_sq2, s_rms2))
                if t >= 1:
                    act.wait_ge(s_h2tp, t)
                    if t >= 3:
                        act.wait_ge(s_rt, t - 2)
                    nc.scalar.activation(hn2T[(t - 1) % 2].rearrange("p a b -> p (a b)"), flat(4, 2), ACT.Copy
                                         ).then_inc(s_h2T, 1)
            act.wait_ge(s_bT, 2)
            nc.scalar.activation(biasT, ps[:, 0, :], ACT.Copy).then_inc(s_bTc, 1)
            nc.scalar.activation(biasdT, ps[:, 1, 0:NE * KD], ACT.Copy).then_inc(s_bTc, 1)
            act.wait_ge(s_gexp, 1)
            nc.scalar.activation(gates, gates, ACT.Exp).then_inc(s_gexpd, 1)

            def place_rows(p, mains, part=range(4)):
                for a in part:
                    act.wait_ge(s_xtp, p * 4 + a + 1)
                    if a == 0 and mains is not None:
                        act.wait_ge(s_gu, mains * FJ)
                    nc.scalar.activation(xgT[:, 2 * a:2 * a + 2, :],
                                         ps[:, 4 + a % 2, 0:2 * CAP].rearrange("p (a b) -> p a b", a=2),
                                         ACT.Copy).then_inc(s_xgT, 1)

            def gate_sigmoids(n):
                for j in range(FJ):
                    act.wait_ge(s_glm, n * 3 * FJ + 3 * j + 1)
                    nc.scalar.activation(sig, gmin, ACT.Sigmoid, scale=ALPHA).then_inc(s_sig, 1)

            def finish_rows(n, e, after_first=None):
                for f in range(KD):
                    act.wait_ge(s_dn, n * KD + f + 1)
                    act.wait_ge(s_ytp, n * KD + max(f, 1))
                    nc.scalar.activation(yT[f % 2], ps[:, 2 + f % 2, 0:CAP], ACT.Identity,
                                         bias=biasdT[:, bass.ds(e * KD + f, 1)]).then_inc(s_yT, 1)
                    if f == 0 and after_first:
                        after_first()

            place_rows(0, None)
            with act.Fori(0, NE) as e:
                gate_sigmoids(e)
                place_rows(e + 1, e + 1, range(2))
                finish_rows(e, e, after_first=lambda: place_rows(e + 1, e + 1, range(2, 4)))
            total = act.value_load(n_items[0:1, 0:1], min_val=0, max_val=EXTRA)
            with act.Fori(0, EXTRA) as i:
                with act.If(total > i):
                    e = read_index(act, item_e, i, NE - 1)
                    place_rows(i + NE + 1, i + NE)
                    gate_sigmoids(i + NE)
                    finish_rows(i + NE, e)
                act.nop()
            act.wait_ge(s_plan, 1)
            for tiles in FINAL_GROUPS:
                for t in tiles:
                    act.wait_ge(s_back[t], 16)
                    if t:
                        act.wait_ge(s_sq3, t)
                    if t == tiles[0] and t:
                        act.wait_ge(s_rms3, FINAL_GROUPS.index(tiles))
                    nc.scalar.activation(junk, h_sb[:, t, :], ACT.Square, accum_out=ssq2[:, t:t + 1]).then_inc(s_sq3, 1)
                c = slice(tiles[0], tiles[-1] + 1)
                act.wait_ge(s_sq3, tiles[-1] + 1)
                nc.scalar.activation(rms2[:, c], ssq2[:, c], ACT.Sqrt, scale=1.0 / D, bias=eps).then_inc(s_rms3, 1)

        def moe_tensor(pe):
            pe.wait_ge(s_wout, 16)
            pe.wait_ge(s_cn, 1)

            def mix(k, t):
                if k < CC:
                    return conv_out(k)[:, t * P:t * P + P]
                return aT[:, k - CC, t * P:t * P + P]

            def turn_hn2(t):
                pe.wait_ge(s_hn2, t + 1)
                if t:
                    pe.wait_ge(s_h2T, t)
                for k in range(KD):
                    last = nc.tensor.transpose(ps[:, 4 + k // 4, (k % 4) * P:(k % 4) * P + P],
                                               hn2[t % 2][:, k * P:k * P + P], ident)
                last.then_inc(s_h2tp, 1)

            def router(t):
                pe.wait_ge(s_h2T, t + 1)
                for k in range(KD):
                    last = nc.tensor.matmul(ps[:, 6, t * NE:t * NE + NE], hn2T[t % 2][:, k, :], w_rt[:, k, :],
                                            start=(k == 0), stop=(k == KD - 1))
                last.then_inc(s_rt, 1)

            for t in range(NT + 2):
                if t < NT:
                    if t >= 2:
                        pe.wait_ge(s_h2, t - 1)
                    pe.wait_ge(s_aT, HEADS if t == 0 else 2 * HEADS)
                    for part in (range(CC, KD), range(CC)):
                        if part[0] == 0 and t % 4 == 0:
                            pe.wait_ge(s_uo, CC * (1 + t // 4))
                        for n in range(2):
                            for k in part:
                                last = nc.tensor.matmul(wo_banks(t)[:, n, :], mix(k, t), wout[:, k, 512 * n:512 * n + 512],
                                                        start=(k == CC), stop=(k == CC - 1))
                    last.then_inc(s_wo, 1)
                if t == 1:
                    pe.wait_ge(s_par, 16 * N_PAR)
                if 1 <= t <= NT:
                    turn_hn2(t - 1)
                if t >= 2:
                    router(t - 2)
            pe.wait_ge(s_bias, 16 * N_BIAS)
            pe.wait_ge(s_h2, NT)
            for bank, rows, n in ((0, bias_gu_rows, 4), (1, bias_d_rows, 2)):
                for a in range(n):
                    last = nc.tensor.transpose(ps[:, bank, a * P:a * P + P], rows[:, a, :], ident)
                last.then_inc(s_bT, 1)
            pe.wait_ge(s_mem, 1)
            for t in range(NT + 1):
                last_of = min(t, NT - 1)
                for s in range(last_of + 1):
                    own = s == t
                    last = nc.tensor.matmul(ps[:, 7, t * NE:t * NE + NE], upperb if own else onesb, member[:, s, :],
                                            start=(s == 0), stop=(s == last_of))
            last.then_inc(s_rank, 1)

            def sum_slots(c0, c1, rows):
                for half, m in ((0, P), (1, CAP2)):
                    c = LIST_AT[half]
                    for t in range(NT):
                        last = nc.tensor.matmul(ps[0:m, 5, c + c0:c + c1], picks[:, t, P * half:P * half + m], rows(t),
                                                start=(t == 0), stop=(t == NT - 1))
                return last

            def list_tokens(p, e):
                pe.wait_ge(s_pick, p + 1)
                pe.wait_ge(s_tok, p * 4)
                sum_slots(0, SLOT_COLS, lambda t: slot_rows[:, t, bass.ds(e, 1), :]).then_inc(s_list, 1)

            def turn_rows(p, part):
                pe.wait_ge(s_gat, p * 32 + 32)
                for a in part:
                    if isinstance(p, int) and p == 0:
                        if a >= 2:
                            pe.wait_ge(s_xgT, a - 1)
                    else:
                        pe.wait_ge(s_xgT, p * 4 + a - 1)
                    for b in range(2):
                        k = 2 * a + b
                        nc.tensor.transpose(ps[:, 4 + a % 2, b * CAP:b * CAP + P], xg[0][:, k * P:k * P + P], ident)
                        last = nc.tensor.transpose(ps[:, 4 + a % 2, b * CAP + P:b * CAP + CAP],
                                                   xg[1][:, k * P:k * P + P], ident[0:CAP2, 0:CAP2])
                    last.then_inc(s_xtp, 1)

            def gate_up(n, p, j, width=CAP):
                if j == 0:
                    pe.wait_ge(s_xgT, p * 4 + 4)
                if j % 2 == 0:
                    pe.wait_ge(s_wgu[j // 2], n * 32 + 32)
                if j >= 2:
                    pe.wait_ge(s_glm, n * 3 * FJ + 3 * (j - 2) + 2)
                for a in range(2):
                    for k in range(KD):
                        last = nc.tensor.matmul(ps[:, j % 2, a * CAP:a * CAP + width],
                                                w_gu[j // 2][:, k, a, P * (j % 2):P * (j % 2) + P], xgT[:, k, 0:width],
                                                start=(k == 0), stop=(k == KD - 1))
                last.then_inc(s_gu, 1)

            def turn_feature(n, f, width=CAP):
                pe.wait_ge(s_yT, n * KD + f + 2)
                c = f % 4
                if c == 0:
                    pe.wait_ge(s_add, n * 4 + 2 * (f // 4) + 1)
                last = nc.tensor.transpose(ps[:, 6, c * P:c * P + P], yT[f % 2][:, 0:P], ident)
                if width > P:
                    last = nc.tensor.transpose(ps[0:CAP2, 7, c * P:c * P + P], yT[f % 2][:, P:CAP], ident)
                last.then_inc(s_ytp, 1)

            def down(n, width=CAP, between=None):
                def product(f, k):
                    return nc.tensor.matmul(ps[:, 2 + f % 2, 0:width], w_dn[f // 2][:, k, P * (f % 2):P * (f % 2) + P],
                                            hT[:, k, 0:width], start=(k == 0), stop=(k == FJ - 1))

                pe.wait_ge(s_wdn[0], n * 16 + 16)
                for k in range(FJ - 1):
                    pe.wait_ge(s_hid, n * FJ + k + 1)
                    for f in range(2):
                        product(f, k)
                pe.wait_ge(s_hid, n * FJ + FJ)
                for f in range(2):
                    product(f, FJ - 1).then_inc(s_dn, 1)
                if between:
                    between()
                for f in range(2, KD + 1):
                    if f == 2:
                        turn_feature(n, 0, width)
                    if f < KD:
                        if f % 2 == 0:
                            pe.wait_ge(s_wdn[f // 2], n * 16 + 16)
                        pe.wait_ge(s_yT, n * KD + f)
                        for k in range(FJ):
                            last = product(f, k)
                        last.then_inc(s_dn, 1)
                        turn_feature(n, f - 1, width)

            pe.wait_ge(s_bTc, 2)
            pe.wait_ge(s_class, 1)
            pe.wait_ge(s_pick, 1)
            sum_slots(0, 2, lambda t: tokb[:, t, :]).then_inc(s_list, 1)
            pe.wait_ge(s_rows, 1)
            pe.wait_ge(s_tok, 2)
            sum_slots(2, SLOT_COLS, lambda t: slot_rows[:, t, 0, 2:SLOT_COLS]).then_inc(s_listg, 1)
            pe.wait_ge(s_tok, 4)
            turn_rows(0, range(4))
            pe.wait_ge(s_add, 1)
            width_class = pe.alloc_register("width_class")
            next_class = pe.alloc_register("next_width_class")
            pe.reg_load(width_class, classes[0:1, 0:1])
            pe.reg_mov(next_class, 0)
            with pe.Fori(0, NE) as e:
                for c, width in enumerate(WIDTHS):
                    with pe.If_eq(width_class, c):
                        for j in range(FJ):
                            gate_up(e, e, j, width)
                            if j == 0:
                                pe.wait_ge(s_yT, e * KD + 1)
                                nc.tensor.transpose(ps[:, 6, 3 * P:4 * P], yT[1][:, 0:P], ident)
                                nc.tensor.transpose(ps[0:CAP2, 7, 3 * P:4 * P], yT[1][:, P:CAP], ident).then_inc(s_ytp, 1)
                            if j == 2:
                                list_tokens(e + 1, e + 1)
                            if j == FJ - 2:
                                turn_rows(e + 1, range(2))
                                pe.reg_load(next_class, classes[0:1, bass.ds(e + 1, 1)])
                        down(e, width, between=lambda: turn_rows(e + 1, range(2, 4)))
                    pe.nop()
                pe.reg_mov(width_class, next_class)
            turn_feature(NE - 1, KD - 1)
            total = pe.value_load(n_items[0:1, 0:1], min_val=0, max_val=EXTRA)
            with pe.Fori(0, EXTRA) as i:
                with pe.If(total > i):
                    list_tokens(i + NE + 1, read_index(pe, item_e, i, NE - 1))
                    turn_rows(i + NE + 1, range(4))
                    for j in range(FJ):
                        gate_up(i + NE, i + NE + 1, j)
                    down(i + NE)
                    turn_feature(i + NE, KD - 1)
                pe.nop()

        def moe_vector(dve, steps, link, refine):
            V = nc.vector
            def take_tokens(half, m):
                c = LIST_AT[half]
                V.tensor_scalar(token_idx[0:m, half:half + 1], ps[0:m, 5, c:c + 1], ps[0:m, 5, c + 1:c + 2],
                                float(SEQ), ALU.add, ALU.add).then_inc(s_tok, 1)

            def take_gates(half, m):
                c = LIST_AT[half]
                V.tensor_scalar(token_gate[0:m, half:half + 1], ps[0:m, 5, c + 2:c + 3], ps[0:m, 5, c + 3:c + 4],
                                ps[0:m, 5, c + 4:c + 5], ALU.add, ALU.add).then_inc(s_tok, 1)

            def take_list(p):
                dve.wait_ge(s_list, p + 1)
                dve.wait_ge(s_gat, p * 32)
                for half, m in ((0, P), (1, CAP2)):
                    take_tokens(half, m)
                    take_gates(half, m)

            dve.wait_ge(s_par, 16 * N_PAR)
            link(V.memset(onesb, 1.0))
            link(V.tensor_copy(upperb, upper))
            for t in range(NT):
                dve.wait_ge(s_wo, t + 1)
                dve.wait_ge(s_xr[t % 3], 16 * (t // 3 + 1))
                V.tensor_tensor(h_sb[:, t, :], wo_banks(t).rearrange("p b n -> p (b n)"), x_again[t % 3], ALU.add).then_inc(s_h2, 1)
                dve.wait_ge(s_h2, t + 1)
                dve.wait_ge(s_rms2, t + 1)
                c = slice(t, t + 1)
                link(V.reciprocal(rstd2[:, c], rms2[:, c]))
                link(V.tensor_scalar(ssq2[:, c], ssq2[:, c], 1.0 / D, EPS, ALU.mult, ALU.add))
                refine(rstd2[:, c], ssq2[:, c], tmp2[:, c])
                if t >= 2:
                    dve.wait_ge(s_h2tp, t - 1)
                    dve.wait_ge(s_hst[t % 2], 16 * (t // 2))
                V.scalar_tensor_tensor(hn2[t % 2], h_sb[:, t, :], rstd2[:, c], gain2, ALU.mult, ALU.mult).then_inc(s_hn2, 1)
            link(V.tensor_copy(tokb, tok))
            for slots in (token_idx, kept_idx, round_idx):
                link(V.memset(slots, 0))
            for slots in (token_gate, kept_gate, round_gate):
                link(V.memset(slots, 0.0))
            V.memset(yT[1], 0.0).then_inc(s_yT, 1)
            V.memset(yT[0], 0.0).then_inc(s_add, 1)
            dve.wait_ge(s_rt, NT)
            link(V.tensor_tensor(logits, ps[:, 6, 0:NT * NE].rearrange("p (t e) -> p t e", t=NT),
                                 b_rt.unsqueeze(1).to_broadcast([P, NT, NE]), ALU.add))
            for t in range(NT):
                link(V.max(top8[:, t, :], logits[:, t, :]))
                link(V.max_index(top8_i[:, t, :], top8[:, t, :], logits[:, t, :]))
            link(V.tensor_copy(top8_f, top8_i))
            V.tensor_tensor(gates, top8[:, :, 0:TOPE], top8[:, :, 0:1].to_broadcast([P, NT, TOPE]), ALU.subtract
                            ).then_inc(s_gexp, 1)
            experts = iota[:, 0:NE].unsqueeze(1).to_broadcast([P, NT, NE])
            for j in range(TOPE):
                link(V.tensor_tensor(onehot[:, j], experts, top8_f[:, :, j:j + 1].to_broadcast([P, NT, NE]), ALU.is_equal))
            link(V.tensor_tensor(member, onehot[:, 0], onehot[:, 1], ALU.add))
            link(V.tensor_tensor(member, member, onehot[:, 2], ALU.add))
            V.tensor_tensor(member, member, onehot[:, 3], ALU.add).then_inc(s_mem, 1)
            dve.wait_ge(s_gexpd, 1)
            link(V.tensor_reduce(tmp2, gates, AX, ALU.add))
            link(V.reciprocal(tmp2, tmp2))
            link(V.tensor_tensor(gates, gates, tmp2.unsqueeze(2).to_broadcast([P, NT, TOPE]), ALU.mult))
            dve.wait_ge(s_rank, 1)
            dve.wait_ge(s_mem, 1)
            rank_ps = ps[:, 7, 0:NT * NE].rearrange("p (t e) -> p t e", t=NT)
            link(V.memset(ranked, -1.0))
            link(V.scalar_tensor_tensor(prod, rank_ps, 1.0, member, ALU.add, ALU.mult))
            link(V.tensor_scalar(ranked[:, :, 0:NE], prod, -1.0, None, ALU.add))
            link(V.tensor_copy(counts, ps[:, 7, NT * NE:NT * NE + NE]))
            link(V.tensor_scalar(extra_rounds, counts, WIDTHS[0] + 0.5, None, ALU.is_gt))
            for w in WIDTHS[1:-1]:
                link(V.tensor_scalar(round_cmp, counts, w + 0.5, None, ALU.is_gt))
                link(V.tensor_tensor(extra_rounds, extra_rounds, round_cmp, ALU.add))
            link(V.memset(classes, 0))
            V.tensor_copy(classes[:, 0:NE], extra_rounds).then_inc(s_class, 1)
            dve.wait_ge(s_class, 1)
            make_picks(dve, 0, ranked[:, :, 0:1])
            dve.wait_ge(s_list, 1)
            for half, m in ((0, P), (1, CAP2)):
                take_tokens(half, m)
            for j in range(TOPE):
                dst = gate_rest if j else gate_of
                link(V.tensor_tensor(dst, onehot[:, j], gates[:, :, j:j + 1].to_broadcast([P, NT, NE]), ALU.mult))
                if j:
                    link(V.tensor_tensor(gate_of, gate_of, gate_rest, ALU.add))
            link(V.memset(slot_rows, 0.0))
            for part in range(3):
                at_part = slot_rows[:, :, 0:NE, 2 + part:3 + part].rearrange("p t e a -> p t (e a)")
                link(V.tensor_copy(at_part, gate_of))
                if part < 2:
                    link(V.tensor_tensor(gate_of, gate_of, at_part, ALU.subtract))
            V.tensor_copy(slot_rows[:, :, 0:NE, 0:2], tok.unsqueeze(2).to_broadcast([P, NT, NE, 2])).then_inc(s_rows, 1)
            link(V.memset(ps[:, 7, :], 0.0))
            dve.wait_ge(s_listg, 1)
            for half, m in ((0, P), (1, CAP2)):
                take_gates(half, m)
            link(V.tensor_scalar(extra_rounds, counts, CAP + 0.5, None, ALU.is_gt))
            for r in range(2, ROUNDS):
                link(V.tensor_scalar(round_cmp, counts, CAP * r + 0.5, None, ALU.is_gt))
                link(V.tensor_tensor(extra_rounds, extra_rounds, round_cmp, ALU.add))
            link(V.tensor_tensor_scan(extra_sum, extra_rounds, extra_rounds, 0.0, ALU.add, ALU.bypass))
            link(V.tensor_copy(n_items, extra_sum[:, NE - 1:NE]))
            link(V.tensor_tensor(item_cmp, extra_sum.unsqueeze(1).to_broadcast([P, EXTRA, NE]),
                                 iota[:, 0:EXTRA].unsqueeze(2).to_broadcast([P, EXTRA, NE]), ALU.is_le))
            link(V.tensor_reduce(item_e_f, item_cmp, AX, ALU.add))
            link(V.tensor_tensor(item_cmp, item_cmp, extra_rounds.unsqueeze(1).to_broadcast([P, EXTRA, NE]), ALU.mult))
            link(V.tensor_reduce(item_x_f, item_cmp, AX, ALU.add))
            link(V.tensor_tensor(item_x_f, iota[:, 0:EXTRA], item_x_f, ALU.subtract))
            link(V.tensor_scalar(item_x_f, item_x_f, 1.0, None, ALU.add))
            link(V.tensor_scalar(item_off, item_x_f, float(CAP), None, ALU.mult))
            link(V.tensor_copy(item_e, item_e_f))
            bias4 = biasT.rearrange("p (e a j) -> p e a j", a=2, j=FJ)
            dve.wait_ge(s_bTc, 2)
            link(V.tensor_scalar(bias4[:, :, 1, :], bias4[:, :, 1, :], 1.0, None, ALU.add))
            V.memset(tmp2, 0.0).then_inc(s_plan, 1)

            def take_round(n, idx, gate):
                dve.wait_ge(s_free, n + 1)
                V.tensor_copy(round_idx, idx).then_inc(s_turn, 1)
                V.tensor_copy(round_gate, gate).then_inc(s_turn, 1)

            def add_rows(n, half):
                dve.wait_ge(s_hg, n * 32 + 32)
                dve.wait_ge(s_ytp, n * KD + 1 + 4 * (half + 1))
                f = slice(512 * half, 512 * half + 512)
                for b, m in ((0, P), (1, CAP2)):
                    V.scalar_tensor_tensor(h_rows[b][:, f], ps[0:m, 6 + b, :], round_gate[0:m, b:b + 1], h_rows[b][:, f],
                                           ALU.mult, ALU.add).then_inc(s_add, 1)

            def swiglu(n, e, j):
                c3 = 3 * j
                dve.wait_ge(s_gu, n * FJ + j + 1)
                if j:
                    dve.wait_ge(s_hid, n * FJ + j)
                V.tensor_scalar(gmin, ps[:, j % 2, 0:CAP], biasT[:, bass.ds(e * 2 * FJ + j, 1)], LIMIT, ALU.add, ALU.min
                                ).then_inc(s_glm, 1)
                V.tensor_scalar(umin, ps[:, j % 2, CAP:2 * CAP], biasT[:, bass.ds(e * 2 * FJ + FJ + j, 1)],
                                LIMIT + 1.0, ALU.add, ALU.min).then_inc(s_glm, 1)
                dve.wait_ge(s_sig, n * FJ + j + 1)
                dve.wait_ge(s_glm, n * 3 * FJ + c3 + 2)
                V.tensor_tensor(gsig, gmin, sig, ALU.mult).then_inc(s_glm, 1)
                dve.wait_ge(s_glm, n * 3 * FJ + c3 + 3)
                V.scalar_tensor_tensor(hT[:, j, :], umin, 1.0 - LIMIT, gsig, ALU.max, ALU.mult).then_inc(s_hid, 1)

            with dve.Fori(0, NE) as e:
                for j in range(FJ):
                    swiglu(e, e, j)
                    if j == 0:
                        make_picks(dve, e + 1, ranked[:, :, bass.ds(e + 1, 1)])
                    if j == 2:
                        dve.wait_ge(s_tok, e * 4 + 4)
                        V.tensor_copy(kept_idx, token_idx).then_inc(s_kept, 1)
                        V.tensor_copy(kept_gate, token_gate).then_inc(s_kept, 1)
                        dve.wait_ge(s_kept, e * 2 + 2)
                        take_list(e + 1)
                    if j == 5:
                        take_round(e, kept_idx, kept_gate)
                add_rows(e, 0)
                add_rows(e, 1)
            total = dve.value_load(n_items[0:1, 0:1], min_val=0, max_val=EXTRA)
            with dve.Fori(0, EXTRA) as i:
                with dve.If(total > i):
                    e = read_index(dve, item_e, i, NE - 1)
                    dve.wait_ge(s_pick, i + NE + 1)
                    V.tensor_scalar(pos_item, ranked[:, :, bass.ds(e, 1)].rearrange("p t a -> p (t a)"),
                                    item_off[:, bass.ds(i, 1)], None, ALU.subtract).then_inc(s_item, 1)
                    dve.wait_ge(s_item, i + 1)
                    make_picks(dve, i + NE + 1, pos_item.unsqueeze(2))
                    dve.wait_ge(s_turn, i * 2 + 2 * NE)
                    take_list(i + NE + 1)
                    dve.wait_ge(s_tok, i * 4 + 4 * (NE + 2))
                    take_round(i + NE, token_idx, token_gate)
                    for j in range(FJ):
                        swiglu(i + NE, e, j)
                    add_rows(i + NE, 0)
                    add_rows(i + NE, 1)
                dve.nop()
            for n, tiles in enumerate(FINAL_GROUPS):
                c = slice(tiles[0], tiles[-1] + 1)
                dve.wait_ge(s_rms3, n + 1)
                link(V.reciprocal(rstd2[:, c], rms2[:, c]))
                link(V.tensor_scalar(ssq2[:, c], ssq2[:, c], 1.0 / D, EPS, ALU.mult, ALU.add))
                refine(rstd2[:, c], ssq2[:, c], tmp2[:, c])
                for t in tiles:
                    V.scalar_tensor_tensor(h_sb[:, t, :], h_sb[:, t, :], rstd2[:, t:t + 1], gainf, ALU.mult, ALU.mult
                                           ).then_inc(s_fin, 1)

        s_class = sem("width_classes_ready")
        s_item = sem("item_positions")

        def make_picks(dve, p, pos):
            if not (isinstance(p, int) and p == 0):
                dve.wait_ge(s_list, p)
            nc.vector.tensor_tensor(picks, iota.unsqueeze(1).to_broadcast([P, NT, CAP]),
                                    pos.to_broadcast([P, NT, CAP]), ALU.is_equal).then_inc(s_pick, 1)

        block = ctx.enter_context(nc.Block())
        N_SMALL, N_CONV = 5, 7

        U_KI, U_QI, U_K, U_V, U_Q = 0, NT, 2 * NT, 3 * NT, 4 * NT
        J_QI, J_K, J_Q, J_M = 2, 2 + NT, 2 + 2 * NT, 2 + 3 * NT

        @block.sync
        def _(sp):
            small = [
                (invf, consts[:, K_INV:K_INV + HALF_HD]),
                (posq_i, positions[0].rearrange("(t p) -> p t", p=P)),
                (pos_row, pos_row_src),
                (lng, idx_k_norm_g[0].partition_broadcast(P)),
                (lnb, idx_k_norm_b[0].partition_broadcast(P)),
            ]
            conv_small = [
                (convb, conv_b[0].rearrange("(c p) -> p c", p=P)),
                (cng, conv_norm_g[0].rearrange("(c p) -> p c", p=P)),
                (cnb, conv_norm_b[0].rearrange("(c p) -> p c", p=P)),
                (convw[:, 0, :], conv_w[0, :, 0:P].rearrange("k p -> p k")),
                (convw[:, 1, :], conv_w[0, :, P:2 * P].rearrange("k p -> p k")),
                (convw[:, 2, :], conv_w[0, :, 2 * P:3 * P].rearrange("k p -> p k")),
                (convw[:, 3, :], conv_w[0, :, 3 * P:4 * P].rearrange("k p -> p k")),
            ]
            sp.dma_start(ident, ident_src).then_inc(s_first, 16)
            with nc.allow_non_contiguous_dma(reason="a gain along partitions"):
                sp.dma_start(gmixT, norm_mix_g[0].rearrange("(k p) -> p k", p=P)).then_inc(s_first, 16)
            for t in range(NT):
                sp.dma_start(x_sb[:, t, :], x_t[t]).then_inc(s_xt[t], 16)
            sp.dma_start(wki, win[:, :, C_KI:C_KI + N_KI]).then_inc(s_w["ki"], 16)
            with nc.allow_non_contiguous_dma(reason="small parameters"):
                for dst, src in small:
                    sp.dma_start(dst, src).then_inc(s_small, 16)
            sp.dma_start(wbuf[0], win[:, :, C_QI:C_QI + 512]).then_inc(s_w["qi"], 16)
            with nc.allow_non_contiguous_dma(reason="parameters of the convolution"):
                for dst, src in conv_small:
                    sp.dma_start(dst, src).then_inc(s_convp, 16)
            sp.wait_ge(s_zero, 1)
            for rows in (xn_dram, h_dram):
                sp.dma_start(rows[SEQ:SEQ + 1, :], zero_rows[0:1]).then_inc(s_zeroed, 16)
            sp.wait_ge(s_proj, U_QI)
            sp.wait_ge(s_zeroed, 32)
            sp.dma_start(wbuf[1], win[:, :, C_CONV:2 * C_CONV]).then_inc(s_w["gate"], 16)
            sp.wait_ge(s_proj, U_K)
            sp.dma_start(wbuf[0], win[:, :, 0:C_CONV]).then_inc(s_w["val"], 16)
            sp.wait_ge(s_idx, NT * HEADS)
            sp.dma_start(w_kvq[0], win[:, :, C_K:C_K + 512]).then_inc(s_w["k"], 16)
            sp.wait_ge(s_glu, 2 * CC)
            sp.dma_start(w_kvq[1], win[:, :, C_V:C_V + 512]).then_inc(s_w["v"], 16)
            sp.dma_start(w_kvq[2], win[:, :, C_Q:C_Q + 512]).then_inc(s_w["q"], 16)
            sp.wait_ge(s_rotB, 2 * NT)
            sp.dma_start(headrow, head_rows).then_inc(s_hrow, 16)
            sp.wait_ge(s_mx, NT * HEADS)
            sp.dma_start(wout, w_out[0].rearrange("(k p) n -> p k n", p=P)).then_inc(s_wout, 16)
            moe_sync(sp)

        @block.scalar
        def _(act):
            for t in range(NT):
                act.wait_ge(s_xt[t], 16)
                if t:
                    act.wait_ge(s_sq, t)
                nc.scalar.activation(junk_x, x_sb[:, t, :], ACT.Square, accum_out=ssq[:, t:t + 1]).then_inc(s_sq, 1)
                if t % 4 == 3:
                    act.wait_ge(s_sq, t + 1)
                    act.wait_ge(s_kis, 1)
                    nc.scalar.activation(rms[:, t - 3:t + 1], ssq[:, t - 3:t + 1], ACT.Sqrt, scale=1.0 / D, bias=eps
                                         ).then_inc(s_rms, 1)
            act.wait_ge(s_first, 32)
            for i in range(2 * KD):
                n, k = i // KD, i % KD
                act.wait_ge(s_htp, i + 1)
                nc.scalar.activation(hnT[:, k, 512 * n:512 * n + 512], ps[:, 4 + i % 4, :], ACT.Identity,
                                     scale=gmixT[:, k:k + 1]).then_inc(s_hnT, 1)
            def copy_proj(u, dst, src):
                act.wait_ge(s_proj, u + 1)
                nc.scalar.activation(dst, src, ACT.Copy).then_inc(s_raw, 1)

            def copy_tp(j, dst, src):
                act.wait_ge(s_tp, j + 1)
                nc.scalar.activation(dst, src, ACT.Copy).then_inc(s_tpv, 1)

            for t in range(NT):
                copy_proj(U_KI + t, kiw[:, t, :], ps[:, t % 2, 0:N_KI])
            act.wait_ge(s_trig, 1)
            nc.scalar.activation(sin2[:, :, HALF_HD:HD], ang_r, ACT.Sin).then_inc(s_sin, 1)
            act.wait_ge(s_trig, 2)
            nc.scalar.activation(cos2[:, :, 0:HALF_HD], ang, ACT.Sin).then_inc(s_sin, 1)

            def tile4(dst, t):
                return dst[:, :, t * P:t * P + P]

            act.wait_ge(s_kivar, 1)
            nc.scalar.activation(kis2, kis1, ACT.Sqrt, scale=1.0 / HD, bias=eps).then_inc(s_kirms, 1)
            for t in range(NT + 2):
                if t < NT:
                    if t >= 2:
                        act.wait_ge(s_rotA, t - 1)
                    copy_proj(U_QI + t, raw[t % 2], ps[:, t % 2, :])
                if t == 1:
                    act.wait_ge(s_kiz, 2)
                    for n in range(2):
                        act.wait_ge(s_tp, n + 1)
                        for b, r in ((0, 0), (1, HD)):
                            last = nc.scalar.activation(ki_pad[b][r:r + HD, 512 * n:512 * n + 512],
                                                        ps[r:r + HD, 2 + n, :], ACT.Copy)
                        last.then_inc(s_tpv, 1)
                if t >= 2:
                    copy_tp(J_QI + t - 2, tile4(qiT, t - 2), ps[:, 2 + t % 2, :].rearrange("p (a b) -> p a b", a=4))
            act.wait_ge(s_causal, 1)
            causal_flag = act.value_load(causal_i[0:1, 0:1], min_val=0, max_val=1)

            def relus(causal):
                for i in range(NT * HEADS):
                    w = keys_of(i // HEADS, causal)
                    act.wait_ge(s_idx, i + 1)
                    if i >= 2:
                        act.wait_ge(s_acc, i - 1)
                    nc.scalar.activation(relu_buf[i % 2][:, 0:w], flat(4 + 2 * (i % 2), 2)[:, 0:w], ACT.Relu
                                         ).then_inc(s_relu, 1)

            either(act, causal_flag, relus)
            for i in range(2 * CC):
                act.wait_ge(s_glu, i + 1)
                if i >= 2:
                    act.wait_ge(s_u, i - 1)
                nc.scalar.activation(raw[i % 2], ps[:, 4 + i % 2, :], ACT.Sigmoid).then_inc(s_gluc, 1)
                nc.scalar.activation(rot[i % 2], ps[:, i % 2, :], ACT.Copy).then_inc(s_gluc, 1)
            act.wait_ge(s_u, 2 * CC)
            act.wait_ge(s_padz, 1 + CC)
            for i in range(3 * NT + 2):
                if i < 3 * NT:
                    t, r = i % NT, rotated(i)
                    if r is None:
                        v_dst = vv[:, t, :, :].rearrange("p a (b c) -> p a b c", b=3)[:, :, 0:3:2, :]
                        copy_proj(U_K + i, v_dst, ps[:, i % 2, :].rearrange("p (a b c) -> p a b c", a=4, b=2))
                    else:
                        if r >= 2:
                            act.wait_ge(s_rotB, r - 1)
                        copy_proj(U_K + i, raw[r % 2], ps[:, i % 2, :])
                if i >= 2 and rotated(i - 2) is not None:
                    t, r = (i - 2) % NT, rotated(i - 2)
                    src = ps[:, 2 + r % 2, :].rearrange("p (a b) -> p a b", a=4)
                    if r == 0:
                        act.wait_ge(s_acc, NT * HEADS)
                    if r < NT:
                        copy_tp(J_K + r, tile4(kT, t), src)
                    else:
                        act.wait_ge(s_tp, J_K + r + 1)
                        act.wait_ge(s_qz, 2)
                        for b, p0 in ((0, 0), (1, HD)):
                            last = nc.scalar.activation(q_pad[b][p0:p0 + HD, :, t * P:t * P + P], src[p0:p0 + HD], ACT.Copy)
                        last.then_inc(s_tpv, 1)

            def attention(causal):
                for t in range(NT):
                    tiles = keys_of(t, causal) // P
                    src = ps[:, 2 + t % 2, :].bitcast(BF16).rearrange("p (a b) -> p a b", a=NT)
                    copy_tp(J_M + t, maskT[:, 0:tiles, t * P:t * P + P], src[:, 0:tiles])
                act.wait_ge(s_tp, J_M + NT + 1)
                act.wait_ge(s_qz, 3)
                nc.scalar.activation(negmaxT[0:24, :], ps[0:24, 2, :].bitcast(BF16), ACT.Copy).then_inc(s_tpv, 1)
                blocks = second_pass(causal)
                for i, (g, kt, skip) in enumerate(blocks):
                    act.wait_ge(s_lb, i + 1)
                    if g >= 2:
                        read = [b for b in blocks if b[0] == g - 2 and b[1] <= kt]
                        if read[-1][1] == max(b[1] for b in blocks if b[0] == g - 2):
                            act.wait_ge(s_head, g - 1)
                        else:
                            act.wait_ge(s_pv, sum(b[:2] <= (g - 2, kt) for b in blocks) - (g - 2))
                    nc.scalar.activation(probT[g % 2][:, kt, skip:512], ps[:, 4 + i % 4, skip:512], ACT.Exp,
                                         scale=HD ** -0.5).then_inc(s_exp, 1)
                    if g == 14 and blocks[i + 1][0] == 15:
                        for c in range(2 * CC):
                            act.wait_ge(s_xc, c + 1)
                            if c >= 2:
                                act.wait_ge(s_cvar, c - 1)
                            nc.scalar.activation(sq_buf[c % 2], conv_view(c), ACT.Square).then_inc(s_csq, 1)
                        for n in range(2):
                            act.wait_ge(s_cvar, CC * (n + 1))
                            nc.scalar.activation(lrstd[:, n, :], ps[:, 2 + n, :], ACT.Sqrt, bias=eps).then_inc(s_cstd, 1)

            either(act, causal_flag, attention)
            act.wait_ge(s_cvar, 2 * CC)
            for i in range(2 * CC):
                act.wait_ge(s_cn, i + 1)
                if i >= 2:
                    act.wait_ge(s_uo, i - 1)
                nc.scalar.activation(sg_buf[i % 2], conv_view(i), ACT.Sigmoid).then_inc(s_csg, 1)
            moe_scalar(act)

        @block.tensor
        def _(pe):
            pe.wait_ge(s_first, 32)
            for i in range(2 * KD):
                n, k = i // KD, i % KD
                pe.wait_ge(s_xn, 4 * (n + 1))
                if i >= 4:
                    pe.wait_ge(s_hnT, i - 3)
                for t in range(4):
                    last = nc.tensor.transpose(ps[:, 4 + i % 4, t * P:t * P + P],
                                               x_sb[:, 4 * n + t, k * P:k * P + P], ident)
                last.then_inc(s_htp, 1)

            def project(u, t, w, n):
                if u < NT:
                    pe.wait_ge(s_hnT, KD * (1 + t // 4))
                if u >= 2:
                    pe.wait_ge(s_raw, u - 1)
                for k in range(KD):
                    last = nc.tensor.matmul(ps[:, u % 2, 0:n], hnT[:, k, t * P:t * P + P], w[:, k, 0:n],
                                            start=(k == 0), stop=(k == KD - 1))
                last.then_inc(s_proj, 1)

            def turn4(j, src):
                if j >= 2:
                    pe.wait_ge(s_tpv, j - 1)
                for a in range(4):
                    last = nc.tensor.transpose(ps[:, 2 + j % 2, a * P:a * P + P], src(a), ident)
                last.then_inc(s_tp, 1)

            pe.wait_ge(s_w["ki"], 16)
            for t in range(NT):
                project(U_KI + t, t, wki, N_KI)
            pe.wait_ge(s_w["qi"], 16)
            for t in range(NT + 2):
                if t < NT:
                    project(U_QI + t, t, wbuf[0], 512)
                if t == 1:
                    pe.wait_ge(s_kin, 1)
                    for n in range(2):
                        turn4(n, lambda a: kin[:, 4 * n + a, :])
                if t >= 2:
                    pe.wait_ge(s_rotA, t - 1)
                    turn4(J_QI + t - 2, lambda a: rot[t % 2][:, a * P:a * P + P])
            pe.wait_ge(s_tpv, J_K)
            pe.wait_ge(s_causal, 1)
            causal_flag = pe.value_load(causal_i[0:1, 0:1], min_val=0, max_val=1)

            def index_products(causal):
                for i in range(NT * HEADS):
                    t, h = i // HEADS, i % HEADS
                    if i >= 2:
                        pe.wait_ge(s_relu, i - 1)
                    for n, k0, w in key_parts(t, causal):
                        last = nc.tensor.matmul(ps[:, 4 + 2 * (i % 2) + n, 0:w], qiT[:, h // 2, t * P:t * P + P],
                                                ki_pad[h % 2][:, k0:k0 + w], start=True, stop=True)
                    last.then_inc(s_idx, 1)

            either(pe, causal_flag, index_products)
            pe.wait_ge(s_w["gate"], 16)
            pe.wait_ge(s_w["val"], 16)
            pe.wait_ge(s_raw, U_K)
            pe.wait_ge(s_relu, NT * HEADS)
            for i in range(2 * CC):
                m, n = i // 2, i % 2
                if i >= 2:
                    pe.wait_ge(s_gluc, 2 * (i - 1))
                for w, bank in ((wbuf[1], 4 + i % 2), (wbuf[0], i % 2)):
                    for k in range(KD):
                        last = nc.tensor.matmul(ps[:, bank, :], w[:, k, m * P:m * P + P],
                                                hnT[:, k, 512 * n:512 * n + 512], start=(k == 0), stop=(k == KD - 1))
                last.then_inc(s_glu, 1)
            pe.wait_ge(s_gluc, 4 * CC)
            for i in range(3 * NT + 2):
                if i % NT == 0 and i < 3 * NT:
                    pe.wait_ge(s_w["kvq"[i // NT]], 16)
                if i < 3 * NT:
                    project(U_K + i, i % NT, w_kvq[i // NT], 512)
                if i >= 2 and rotated(i - 2) is not None:
                    r = rotated(i - 2)
                    pe.wait_ge(s_rotB, r + 1)
                    turn4(J_K + r, lambda a: rot[r % 2][:, a * P:a * P + P])
            pe.wait_ge(s_ident, 1)

            def logits_a(causal):
                for t in range(NT):
                    pe.wait_ge(s_mask, t + 1)
                    j = J_M + t
                    pe.wait_ge(s_tpv, j - 1)
                    for a in range(keys_of(t, causal) // P):
                        last = nc.tensor.transpose(ps[:, 2 + j % 2, :].bitcast(BF16)[:, a * P:a * P + P],
                                                   maskq[t][:, a * P:a * P + P], identb)
                    last.then_inc(s_tp, 1)
                    for h in range(HEADS):
                        i = t * HEADS + h
                        if i >= 2:
                            pe.wait_ge(s_mx, i - 1)
                        for n, k0, w in key_parts(t, causal):
                            bank = ps[:, 4 + 2 * (i % 2) + n, 0:w]
                            nc.tensor.matmul(bank, identb, maskq[t][:, k0:k0 + w], start=True, stop=False)
                            last = nc.tensor.matmul(bank, q_pad[h % 2][:, h // 2, t * P:t * P + P],
                                                    kT[:, h // 2, k0:k0 + w], start=False, stop=True)
                        last.then_inc(s_la, 1)
                pe.wait_ge(s_nm, 1)
                pe.wait_ge(s_tpv, J_M + NT)
                for t in range(NT):
                    last = nc.tensor.transpose(ps[0:24, 2, :].bitcast(BF16)[:, t * P:t * P + P],
                                               nm_parts[:, t, :, :].rearrange("p a b -> p (a b)"), identb)
                last.then_inc(s_tp, 1)
                pe.wait_ge(s_tpv, J_M + NT + 1)
                pe.wait_ge(s_hrow, 16)
                pe.wait_ge(s_mx, NT * HEADS)
                pe.wait_ge(s_raw, 5 * NT)

            def logits_b(i, g, kt, skip):
                n, h = g // HEADS, g % HEADS
                bank = ps[:, 4 + i % 4, skip:512]
                if i >= 4:
                    pe.wait_ge(s_exp, i - 3)
                q0, q1 = 512 * n + skip, 512 * n + 512
                nc.tensor.matmul(bank, identb, maskT[:, kt, q0:q1], start=True, stop=False)
                nc.tensor.matmul(bank, headrow[:, h, :], negmaxT[:, q0:q1], start=False, stop=False)
                nc.tensor.matmul(bank, kT[:, h // 2, kt * P:kt * P + P], q_pad[h % 2][:, h // 2, q0:q1],
                                 start=False, stop=True).then_inc(s_lb, 1)

            def weigh_v(i, g, kt, skip, last_kt):
                h = g % HEADS
                c0 = HD * (h % 2)
                pe.wait_ge(s_exp, i + 1)
                if g >= 2 and kt == 0:
                    pe.wait_ge(s_aT, g - 1)
                mm = nc.tensor.matmul(ps[:, g % 2, skip:512], vv[:, kt, h // 2, c0:c0 + P], probT[g % 2][:, kt, skip:512],
                                      start=(kt == 0), stop=(kt == last_kt), skip_group_check=True)
                mm.then_inc(s_head if kt == last_kt else s_pv, 1)

            def conv_stat(square):
                for i in range(2 * CC):
                    n, c = i // CC, i % CC
                    if square:
                        pe.wait_ge(s_csq, i + 1)
                        if i == 0:
                            pe.wait_ge(s_xc, 2 * CC)
                    src = sq_buf[i % 2] if square else conv_view(i)
                    last = nc.tensor.matmul(ps[:, 2 + n, :], ones_c, src, start=(c == 0), stop=(c == CC - 1))
                    if square:
                        last.then_inc(s_cvar, 1)
                if not square:
                    last.then_inc(s_mean, 1)

            def attention(causal):
                logits_a(causal)
                blocks = second_pass(causal)
                by_head = [[(i, *b) for i, b in enumerate(blocks) if b[0] == g] for g in range(2 * HEADS)] + [[]]
                for g in range(2 * HEADS + 1):
                    ahead, behind = by_head[g], by_head[g - 1] if g else []
                    for x in range(NT):
                        if x < len(ahead):
                            logits_b(*ahead[x])
                        if x < len(behind):
                            weigh_v(*behind[x], behind[-1][2])
                    if g == 13:
                        pe.wait_ge(s_conv, CC)
                        conv_stat(False)
                    if g == 14:
                        conv_stat(True)

            either(pe, causal_flag, attention)
            moe_tensor(pe)

        @block.gpsimd
        def _(pool):
            steps = [0]

            def link(ins):
                steps[0] += 1
                ins.then_inc(s_gps, 1)
                pool.wait_ge(s_gps, steps[0])

            nc.gpsimd.memset(eps, EPS).then_inc(s_kis, 1)
            nc.gpsimd.memset(zero_rows, 0.0).then_inc(s_zero, 1)
            nc.gpsimd.memset(vv[:, :, :, HD:2 * HD], 1.0).then_inc(s_padz, 1)
            for c in range(CC):
                nc.gpsimd.memset(cslot[c + 1][:, 0:PAD], 0.0).then_inc(s_padz, 1)
            nc.gpsimd.memset(ki_pad[0], 0.0).then_inc(s_kiz, 1)
            pool.wait_ge(s_trig, 1)
            nc.gpsimd.memset(ki_pad[1], 0.0).then_inc(s_kiz, 1)
            for i in range(2 * CC):
                m, n = i // 2, i % 2
                pool.wait_ge(s_gluc, 2 * (i + 1))
                nc.gpsimd.tensor_tensor(cslot[m + 1][:, PAD + 512 * n:PAD + 512 * n + 512], raw[i % 2], rot[i % 2],
                                        ALU.mult).then_inc(s_u, 1)
            pool.wait_ge(s_acc, NT * HEADS)
            nc.gpsimd.memset(q_pad[0], 0.0).then_inc(s_qz, 1)
            for r in range(2 * NT):
                if r == NT:
                    pool.wait_ge(s_proj, U_Q)
                    nc.gpsimd.memset(q_pad[1], 0.0).then_inc(s_qz, 1)
                pool.wait_ge(s_raw, (U_K if r < NT else U_Q - NT) + r + 1)
                if r:
                    pool.wait_ge(s_rotB, r)
                if r >= 2:
                    pool.wait_ge(s_tp, J_K + r - 1)
                rotate(nc.gpsimd, link, raw[r % 2], rot[r % 2], r % NT).then_inc(s_rotB, 1)
            pool.wait_ge(s_mask, NT)
            nc.gpsimd.memset(negmaxT, 0.0).then_inc(s_qz, 1)
            moe_gpsimd(pool)

        @block.vector
        def _(dve):
            steps = [0]
            V = nc.vector

            def link(ins):
                steps[0] += 1
                ins.then_inc(s_dve, 1)
                dve.wait_ge(s_dve, steps[0])

            def refine(r, mean, tmp):
                link(V.tensor_tensor(tmp, r, r, ALU.mult))
                link(V.tensor_tensor(tmp, tmp, mean, ALU.mult))
                link(V.tensor_scalar(tmp, tmp, -0.5, 1.5, ALU.mult, ALU.add))
                link(V.tensor_tensor(r, r, tmp, ALU.mult))

            for half in range(2):
                c = slice(4 * half, 4 * half + 4)
                dve.wait_ge(s_rms, half + 1)
                link(V.reciprocal(rstd[:, c], rms[:, c]))
                link(V.tensor_scalar(ssq[:, c], ssq[:, c], 1.0 / D, EPS, ALU.mult, ALU.add))
                refine(rstd[:, c], ssq[:, c], rms[:, c])
                for t in range(4 * half, 4 * half + 4):
                    V.tensor_scalar(x_sb[:, t, :], x_sb[:, t, :], rstd[:, t:t + 1], None, ALU.mult).then_inc(s_xn, 1)
            dve.wait_ge(s_first, 32)
            dve.wait_ge(s_small, 16 * N_SMALL)
            V.tensor_copy(identb, ident).then_inc(s_ident, 1)
            link(V.tensor_copy(posq, posq_i))
            link(V.tensor_scalar(posq_i, posq_i, CHUNK_SHIFT, None, ALU.arith_shift_right))
            link(V.tensor_copy(chunk_q, posq_i))
            link(V.tensor_scalar(pos_row, pos_row, CHUNK_SHIFT, None, ALU.arith_shift_right))
            link(V.tensor_copy(chunk_row, pos_row))
            by_tile = chunk_row.rearrange("p (t c) -> p t c", t=NT)
            link(V.tensor_reduce(tile_lo, by_tile, AX, ALU.min))
            link(V.tensor_reduce(tile_hi, by_tile, AX, ALU.max))
            link(V.tensor_tensor(tile_hi[:, 0:NT - 1], tile_hi[:, 0:NT - 1], tile_lo[:, 1:NT], ALU.is_lt))
            link(V.tensor_reduce(tile_lo[:, 0:1], tile_hi[:, 0:NT - 1], AX, ALU.min))
            V.tensor_copy(causal_i, tile_lo[:, 0:1]).then_inc(s_causal, 1)
            dve.wait_ge(s_causal, 1)
            causal_flag = dve.value_load(causal_i[0:1, 0:1], min_val=0, max_val=1)
            for t in range(NT):
                link(V.tensor_scalar(ang[:, t, :], invf, posq[:, t:t + 1], None, ALU.mult))
            for quarter in (0.0, 0.25):
                dst = ang_r if quarter == 0.0 else ang
                link(V.tensor_scalar(turn, ang, 1.0 / TWO_PI, quarter, ALU.mult, ALU.add))
                link(V.tensor_scalar(turn, turn, ROUND_MAGIC, None, ALU.add))
                link(V.tensor_scalar(turn, turn, ROUND_MAGIC, None, ALU.subtract))
                link(V.scalar_tensor_tensor(dst, turn, -PI_A, ang, ALU.mult, ALU.add))
                link(V.scalar_tensor_tensor(dst, turn, -PI_B, dst, ALU.mult, ALU.add))
                link(V.scalar_tensor_tensor(dst, turn, -PI_C, dst, ALU.mult, ALU.add))
                if quarter:
                    link(V.tensor_scalar(dst, dst, np.pi / 2, None, ALU.add))
                V.tensor_scalar(dst, dst, PI_SAFE, -PI_SAFE, ALU.min, ALU.max).then_inc(s_trig, 1)
            dve.wait_ge(s_sin, 2)
            link(V.tensor_scalar(sin2[:, :, 0:HALF_HD], sin2[:, :, HALF_HD:HD], -1.0, None, ALU.mult))
            link(V.tensor_copy(cos2[:, :, HALF_HD:HD], cos2[:, :, 0:HALF_HD]))
            dve.wait_ge(s_raw, NT)
            ki = kiw[:, :, 0:HD]
            link(V.tensor_scalar(wis, kiw[:, :, HD:N_KI], WI_SCALE, None, ALU.mult))
            link(V.tensor_reduce(kis1, ki, AX, ALU.add))
            link(V.tensor_scalar(kis1, kis1, 1.0 / HD, None, ALU.mult))
            link(V.tensor_tensor(kit1, ki, kis1.unsqueeze(2).to_broadcast([P, NT, HD]), ALU.subtract))
            link(V.tensor_tensor(kit2, kit1, kit1, ALU.mult))
            V.tensor_reduce(kis1, kit2, AX, ALU.add).then_inc(s_kivar, 1)
            dve.wait_ge(s_kirms, 1)
            link(V.tensor_scalar(chunk_tmp, kis1, 1.0 / HD, EPS, ALU.mult, ALU.add))
            link(V.reciprocal(kis1, kis2))
            refine(kis1, chunk_tmp, kis2)
            link(V.tensor_tensor(kit1, kit1, kis1.unsqueeze(2).to_broadcast([P, NT, HD]), ALU.mult))
            link(V.tensor_tensor(kit1, kit1, lng.unsqueeze(1).to_broadcast([P, NT, HD]), ALU.mult))
            link(V.tensor_tensor(kit1, kit1, lnb.unsqueeze(1).to_broadcast([P, NT, HD]), ALU.add))
            link(V.tensor_tensor(kit2[:, :, 0:HALF_HD], kit1[:, :, HALF_HD:HD], sin2[:, :, 0:HALF_HD], ALU.mult))
            link(V.tensor_tensor(kit2[:, :, HALF_HD:HD], kit1[:, :, 0:HALF_HD], sin2[:, :, HALF_HD:HD], ALU.mult))
            link(V.tensor_tensor(kit1, kit1, cos2, ALU.mult))
            link(V.tensor_tensor(kin[:, :, 0:HD], kit1, kit2, ALU.add))
            V.tensor_copy(kin[:, :, HD:P], kin[:, :, 0:HD]).then_inc(s_kin, 1)
            for t in range(NT):
                dve.wait_ge(s_raw, U_QI + t + 1)
                if t:
                    dve.wait_ge(s_rotA, t)
                if t >= 2:
                    dve.wait_ge(s_tp, J_QI + t - 1)
                rotate(V, link, raw[t % 2], rot[t % 2], t).then_inc(s_rotA, 1)
            def middle(causal):
                dve.wait_ge(s_htp, 2 * KD)
                for t in range(NT):
                    w = keys_of(t, causal)
                    link(V.tensor_scalar(score[:, t, 0:w], chunk_row[:, 0:w], chunk_q[:, t:t + 1], NOT_ADMITTED, ALU.is_gt, ALU.mult))
                for i in range(NT * HEADS):
                    t, h = i // HEADS, i % HEADS
                    dve.wait_ge(s_relu, i + 1)
                    if i:
                        dve.wait_ge(s_acc, i)
                    w = keys_of(t, causal)
                    V.scalar_tensor_tensor(score[:, t, 0:w], relu_buf[i % 2][:, 0:w], wis[:, t, h:h + 1], score[:, t, 0:w],
                                           ALU.mult, ALU.add).then_inc(s_acc, 1)
                dve.wait_ge(s_acc, NT * HEADS)

                tallies = [0]

                def tally(bits, op):
                    for t in ranked_tiles:
                        w = keys_of(t, causal)
                        tallies[0] += 1
                        if tallies[0] > 2:
                            dve.wait_ge(s_tally, tallies[0] - 2)
                        V.tensor_scalar((ranks.bitcast(BF16), selg)[t % 2][:, 0:w], score[:, t, 0:w], bits[:, t:t + 1], None, op, ALU.add,
                                        accum_out=count[:, t:t + 1]).then_inc(s_tally, 1)
                    dve.wait_ge(s_tally, tallies[0])

                ranked_tiles = [t for t in range(NT) if keys_of(t, causal) > TOPK]
                link(V.memset(count, 0.0))
                link(V.memset(bound, 0))
                tally(bound.bitcast(F32), ALU.is_ge)
                link(V.tensor_scalar(keep, count, TOPK - 0.5, -1.0, ALU.is_lt, ALU.mult))
                link(V.tensor_copy(bound, keep))
                link(V.tensor_scalar(bound_try, bound, 1 << 30, None, ALU.bitwise_xor))
                for b in range(30, -1, -1):
                    tally(bound_try.bitcast(F32), ALU.is_ge)
                    link(V.tensor_scalar(keep, count, TOPK - 0.5, float(1 << b), ALU.is_ge, ALU.mult))
                    link(V.tensor_tensor(bound, bound, keep, ALU.bitwise_xor))
                    if b:
                        link(V.tensor_scalar(bound_try, bound, 1 << (b - 1), None, ALU.bitwise_xor))
                boundf = bound.bitcast(F32)
                dve.wait_ge(s_u, 2 * CC)
                def conv_steps():
                    for c in range(CC):
                        src, dst = cslot[c + 1], conv_out(c)
                        w = convw[:, c, :]
                        link(V.tensor_scalar(dst, src[:, 0:SEQ], w[:, 0:1], convb[:, c:c + 1], ALU.mult, ALU.add))
                        yield
                        for k in range(1, TAPS):
                            ins = V.scalar_tensor_tensor(dst, src[:, k:k + SEQ], w[:, k:k + 1], dst, ALU.mult, ALU.add)
                            link(ins)
                            if k == TAPS - 1:
                                V.tensor_copy(kis2, kis1).then_inc(s_conv, 1)
                            yield

                conv = conv_steps()
                dve.wait_ge(s_padz, 1 + CC)
                dve.wait_ge(s_convp, 16 * N_CONV)
                for t in range(NT):
                    w = keys_of(t, causal)
                    if t not in ranked_tiles:
                        link(V.tensor_scalar(selg[:, 0:w], score[:, t, 0:w], -1.0e38, None, ALU.is_gt))
                        V.tensor_scalar(maskq[t][:, 0:w], selg[:, 0:w], -MASKED, MASKED, ALU.mult, ALU.add).then_inc(s_mask, 1)
                        dve.wait_ge(s_mask, t + 1)
                        continue
                    link(V.tensor_scalar(selg[:, 0:w], score[:, t, 0:w], boundf[:, t:t + 1], None, ALU.is_gt, ALU.add,
                                         accum_out=count[:, t:t + 1]))
                    link(V.tensor_scalar(count[:, t:t + 1], count[:, t:t + 1], -1.0, float(TOPK), ALU.mult, ALU.add))
                    link(V.tensor_scalar(sele[:, 0:w], score[:, t, 0:w], boundf[:, t:t + 1], None, ALU.is_equal))
                    link(V.tensor_tensor_scan(ranks[:, 0:w], sele[:, 0:w], sele[:, 0:w], 0.0, ALU.add, ALU.bypass))
                    link(V.scalar_tensor_tensor(sele[:, 0:w], ranks[:, 0:w], count[:, t:t + 1], sele[:, 0:w], ALU.is_le, ALU.mult))
                    link(V.tensor_tensor(sele[:, 0:w], sele[:, 0:w], selg[:, 0:w], ALU.add))
                    link(V.scalar_tensor_tensor(selg[:, 0:w], score[:, t, 0:w], -1.0e38, sele[:, 0:w], ALU.is_gt, ALU.mult))
                    V.tensor_scalar(maskq[t][:, 0:w], selg[:, 0:w], -MASKED, MASKED, ALU.mult, ALU.add).then_inc(s_mask, 1)
                    dve.wait_ge(s_mask, t + 1)
                for _ in range(CONV_AHEAD[causal][0]):
                    next(conv, None)
                for i in range(NT * HEADS):
                    t, h = i // HEADS, i % HEADS
                    dve.wait_ge(s_la, i + 1)
                    V.tensor_reduce(rowmax[:, t, h:h + 1], flat(4 + 2 * (i % 2), 2)[:, 0:keys_of(t, causal)], AX, ALU.max).then_inc(s_mx, 1)
                    if causal and (t >= 6 or (t >= 3 and h % 2)):
                        next(conv, None)
                dve.wait_ge(s_mx, NT * HEADS)
                dve.wait_ge(s_tp, J_M)
                link(V.tensor_scalar(negmax, rowmax, -1.0, None, ALU.mult))
                link(V.tensor_copy(nm_parts[:, :, 0, :], negmax))
                link(V.tensor_tensor(nm_rest, negmax, nm_parts[:, :, 0, :], ALU.subtract))
                link(V.tensor_copy(nm_parts[:, :, 1, :], nm_rest))
                link(V.tensor_tensor(nm_rest, nm_rest, nm_parts[:, :, 1, :], ALU.subtract))
                V.tensor_copy(nm_parts[:, :, 2, :], nm_rest).then_inc(s_nm, 1)
                link(V.memset(ones_c, 1.0 / C_CONV))

                for g in range(2 * HEADS):
                    if g < 13:
                        for _ in range(CONV_AHEAD[causal][1 + g // HEADS]):
                            next(conv, None)
                    h, n = g % HEADS, g // HEADS
                    r, rd = HD * (h % 2), HD * (1 - h % 2)
                    if g == 13:
                        dve.wait_ge(s_mean, 1)
                        for i in range(2 * CC):
                            V.tensor_tensor(conv_view(i), conv_view(i), ps[:, 2 + i // CC, :], ALU.subtract).then_inc(s_xc, 1)
                    if g == 14:
                        dve.wait_ge(s_xc, 2 * CC)
                        dve.wait_ge(s_cstd, 2)
                        flat_std = lrstd.rearrange("p a b -> p (a b)")
                        link(V.reciprocal(flat_std, flat_std))
                        for i in range(2 * CC):
                            link(V.tensor_tensor(conv_view(i), conv_view(i), lrstd[:, i // CC, :], ALU.mult))
                            V.tensor_scalar(conv_view(i), conv_view(i), cng[:, i % CC:i % CC + 1], cnb[:, i % CC:i % CC + 1],
                                            ALU.mult, ALU.add).then_inc(s_cn, 1)
                    dve.wait_ge(s_head, g + 1)
                    link(V.reciprocal(rden[r:r + HD, :], ps[rd:rd + HD, g % 2, :]))
                    V.tensor_tensor(aT[r:r + HD, h // 2, 512 * n:512 * n + 512], ps[r:r + HD, g % 2, :],
                                    rden[r:r + HD, :], ALU.mult).then_inc(s_aT, 1)

            before = steps[0]
            with dve.If(causal_flag == 0):
                middle(False)
            dve.nop()
            after = steps[0]
            steps[0] = before
            with dve.If(causal_flag == 1):
                middle(True)
                dve.sem_inc(s_dve, after - steps[0])
            dve.nop()
            assert after > steps[0]
            steps[0] = after
            for i in range(2 * CC):
                dve.wait_ge(s_csg, i + 1)
                V.tensor_tensor(conv_view(i), conv_view(i), sg_buf[i % 2], ALU.mult).then_inc(s_uo, 1)
            moe_vector(dve, steps, link, refine)


_INS = ['x', 'positions', 'norm_mix_g', 'w_in', 'idx_k_norm_g', 'idx_k_norm_b', 'conv_w', 'conv_b',
        'conv_norm_g', 'conv_norm_b', 'w_out', 'norm_ffn_g', 'w_router', 'b_router', 'w_gate_up',
        'b_gate_up', 'w_down', 'b_down', 'norm_final_g']


def shape_constants():
    table = np.zeros((P, K_COLS), np.float32)
    table[:, K_IDENT:K_IDENT + P] = np.eye(P)
    table[:, K_UPPER:K_UPPER + P] = np.triu(np.ones((P, P)), 1)
    table[:, K_IOTA:K_IOTA + CAP] = np.arange(CAP)
    half = np.arange(HALF_HD, dtype=np.float32) / np.float32(HALF_HD)
    table[:, K_INV:K_INV + HALF_HD] = np.float32(THETA) ** -half
    table[:, K_TOK:K_TOK + 2 * NT:2] = np.arange(P)[:, None]
    table[:, K_TOK + 1:K_TOK + 2 * NT:2] = P * np.arange(NT) - SEQ
    rows = np.zeros((P, HEADS, P), np.float32)
    for h in range(HEADS):
        rows[h:3 * HEADS:HEADS, h, :] = 1.0
    return table, rows


def kernel(**inputs):
    import ml_dtypes
    import concourse.bacc as bacc
    from concourse.bass_utils import run_bass_kernel_spmd

    nc = bacc.Bacc("TRN2", target_bir_lowering=False, num_devices=1)
    table, rows = shape_constants()
    arrays, args = {}, []
    given = {n: np.ascontiguousarray(inputs[n]) for n in _INS}
    given["consts"] = table
    given["head_rows"] = rows.astype(ml_dtypes.bfloat16)
    for name, a in given.items():
        arrays[f"in_{name}"] = a
        args.append(nc.dram_tensor(f"in_{name}", a.shape, mybir.dt.from_np(a.dtype), kind="ExternalInput").ap())
    args.append(nc.dram_tensor("out_y", (1, SEQ, D), F32, kind="ExternalOutput").ap())
    build(nc, *args)
    r = run_bass_kernel_spmd(nc, [arrays], core_ids=[0])
    return r.results[0]["out_y"]
```
